# Optimizing a Trainium2 kernel written in Bass

```python
import jax, jax.numpy as jnp
from jax import lax
import numpy as np

D_MODEL = 1024
BATCH = 1
SEQ = 512
DEPTH = 1

CTX_LEN = 256
GRID_W = 64
NA_HEADS = 8
HEAD_DIM = 64
NA_WIDTH = NA_HEADS * HEAD_DIM
NA_WIN_ROWS = 8
NA_WIN_COLS = 16
GM_GROUPS = 8
GM_CHUNK = 128
GM_WIDTH = D_MODEL // 2
GM_GROUP_DIM = GM_WIDTH // GM_GROUPS
PEER_HEADS = 8
PEER_N_KEYS = 128
PEER_EXPERTS = PEER_N_KEYS * PEER_N_KEYS
PEER_TOPK = 16
PEER_QDIM = 256
PEER_HALF = PEER_QDIM // 2
PEER_BLOCK = 128
ADA_CHUNKS = 6
EPS = 1e-6
NEG_INF = -1e30
IN_SPLITS = (NA_WIDTH, 2 * NA_WIDTH, 3 * NA_WIDTH, 3 * NA_WIDTH + GM_WIDTH,
             3 * NA_WIDTH + 2 * GM_WIDTH, 3 * NA_WIDTH + 2 * GM_WIDTH + D_MODEL)
IN_COLS = 3 * NA_WIDTH + 2 * GM_WIDTH + 2 * D_MODEL


def rmsnorm(x, g):
    xf = x.astype(jnp.float32)
    y = xf * lax.rsqrt(jnp.mean(xf * xf, axis=-1, keepdims=True) + EPS)
    return (y * g.astype(jnp.float32)).astype(x.dtype)

def layernorm(x, g):
    xf = x.astype(jnp.float32)
    xc = xf - jnp.mean(xf, axis=-1, keepdims=True)
    y = xc * lax.rsqrt(jnp.mean(xc * xc, axis=-1, keepdims=True) + EPS)
    return (y * g.astype(jnp.float32)).astype(x.dtype)

def modulate(h, shift, scale):
    return h * (1 + scale) + shift

def heads(z):
    return z.reshape(z.shape[:-1] + (NA_HEADS, HEAD_DIM))

def neighborhood_attention(q, k, v, k_ctx, v_ctx, rpb):
    B, S = q.shape[0], q.shape[1]
    rows = S // GRID_W
    kh = min(NA_WIN_ROWS, rows)
    band = kh * GRID_W
    scale = HEAD_DIM ** -0.5
    qg = q.reshape(B, rows, GRID_W, NA_HEADS, HEAD_DIM)
    kg = k.reshape(B, rows, GRID_W, NA_HEADS, HEAD_DIM)
    vg = v.reshape(B, rows, GRID_W, NA_HEADS, HEAD_DIM)
    col = jnp.arange(GRID_W)
    col_start = jnp.clip(col - NA_WIN_COLS // 2, 0, GRID_W - NA_WIN_COLS)
    col_in = (col[None, :] >= col_start[:, None]) & (col[None, :] < col_start[:, None] + NA_WIN_COLS)
    band_mask = jnp.broadcast_to(col_in[:, None, :], (GRID_W, kh, GRID_W)).reshape(GRID_W, band)
    dc_idx = jnp.clip(col[None, :] - col[:, None] + NA_WIN_COLS - 1, 0, 2 * NA_WIN_COLS - 2)

    def row_step(r):
        rs = jnp.clip(r - NA_WIN_ROWS // 2, 0, rows - kh)
        q_r = lax.dynamic_index_in_dim(qg, r, axis=1, keepdims=False)
        k_b = lax.dynamic_slice_in_dim(kg, rs, kh, axis=1).reshape(B, band, NA_HEADS, HEAD_DIM)
        v_b = lax.dynamic_slice_in_dim(vg, rs, kh, axis=1).reshape(B, band, NA_HEADS, HEAD_DIM)
        dr_idx = rs + jnp.arange(kh) - r + NA_WIN_ROWS - 1
        bias = rpb[:, dr_idx][:, :, dc_idx]
        bias = bias.transpose(0, 2, 1, 3).reshape(NA_HEADS, GRID_W, band).astype(jnp.float32)
        s_loc = jnp.einsum('bqhd,bkhd->bhqk', q_r, k_b).astype(jnp.float32) * scale + bias
        s_loc = jnp.where(band_mask, s_loc, NEG_INF)
        s_ctx = jnp.einsum('bqhd,bchd->bhqc', q_r, k_ctx).astype(jnp.float32) * scale
        p = jax.nn.softmax(jnp.concatenate([s_loc, s_ctx], axis=-1), axis=-1).astype(v.dtype)
        return (jnp.einsum('bhqk,bkhd->bqhd', p[..., :band], v_b)
                + jnp.einsum('bhqc,bchd->bqhd', p[..., band:], v_ctx))

    o = lax.map(row_step, jnp.arange(rows))
    return jnp.moveaxis(o, 0, 1).reshape(B, S, NA_WIDTH)

def context_attention(q, k, v):
    s = jnp.einsum('bqhd,bkhd->bhqk', q, k).astype(jnp.float32) * (HEAD_DIM ** -0.5)
    p = jax.nn.softmax(s, axis=-1).astype(v.dtype)
    o = jnp.einsum('bhqk,bkhd->bqhd', p, v)
    return o.reshape(o.shape[0], o.shape[1], NA_WIDTH)

def spatial_gating(gu, gv, ln_g, ws, bs):
    B, L, _ = gv.shape
    n = L // GM_CHUNK
    u = jax.nn.gelu(gu)
    vn = layernorm(jax.nn.gelu(gv), ln_g)
    vg = vn.reshape(B, n, GM_CHUNK, GM_GROUPS, GM_GROUP_DIM)
    mixed = jnp.einsum('gpq,bnqgd->bnpgd', ws, vg) + bs.T[:, :, None]
    return u * mixed.reshape(B, L, GM_WIDTH)

def merge_branches(y_a, y_b, ga, gb, w_pa, w_pb, w_out):
    m = jax.nn.sigmoid(ga) * (y_a @ w_pa) + jax.nn.sigmoid(gb) * (y_b @ w_pb)
    return m @ w_out

def peer_ffn(h, wq, sub_keys, expert_u, expert_v):
    B, L, D = h.shape
    blocks = h.reshape(B * L // PEER_BLOCK, PEER_BLOCK, D)

    def block(xb):
        q = (xb @ wq).reshape(PEER_BLOCK, PEER_HEADS, 2, PEER_HALF)
        s = jnp.einsum('thpd,hpkd->thpk', q, sub_keys).astype(jnp.float32)
        s_top, i_top = lax.top_k(s, PEER_TOPK)
        cand_s = (s_top[:, :, 0, :, None] + s_top[:, :, 1, None, :]).reshape(PEER_BLOCK, PEER_HEADS, PEER_TOPK * PEER_TOPK)
        cand_i = (i_top[:, :, 0, :, None] * PEER_N_KEYS + i_top[:, :, 1, None, :]).reshape(PEER_BLOCK, PEER_HEADS, PEER_TOPK * PEER_TOPK)
        best_s, best_pos = lax.top_k(cand_s, PEER_TOPK)
        experts = jnp.take_along_axis(cand_i, best_pos, axis=-1)
        g = jax.nn.softmax(best_s, axis=-1)
        act = jax.nn.gelu(jnp.einsum('thkd,td->thk', expert_u[experts], xb).astype(jnp.float32))
        wgt = (g * act).astype(xb.dtype)
        return jnp.einsum('thk,thkd->td', wgt, expert_v[experts])

    return lax.map(block, blocks).reshape(B, L, D)

def first_inputs(seed: int = 0) -> dict:
    key = jax.random.key(seed)
    ks = jax.random.split(key, 21)
    nrm = jax.random.normal
    return {
        'x': nrm(ks[0], (BATCH, SEQ, D_MODEL), jnp.float32),
        'c': nrm(ks[1], (BATCH, D_MODEL), jnp.float32),
        'ctx': nrm(ks[2], (BATCH, CTX_LEN, D_MODEL), jnp.float32),
        'c_ctx': nrm(ks[3], (D_MODEL,), jnp.float32),
        'ada_w': nrm(ks[4], (DEPTH, D_MODEL, ADA_CHUNKS * D_MODEL), jnp.float32) * (0.3 * D_MODEL ** -0.5),
        'ada_b': nrm(ks[5], (DEPTH, ADA_CHUNKS * D_MODEL), jnp.float32) * 0.02,
        'norm1_g': 1.0 + 0.01 * nrm(ks[6], (DEPTH, D_MODEL), jnp.float32),
        'norm2_g': 1.0 + 0.01 * nrm(ks[7], (DEPTH, D_MODEL), jnp.float32),
        'w_in': nrm(ks[8], (DEPTH, D_MODEL, IN_COLS), jnp.float32) * D_MODEL ** -0.5,
        'na_rpb': nrm(ks[9], (DEPTH, NA_HEADS, 2 * NA_WIN_ROWS - 1, 2 * NA_WIN_COLS - 1), jnp.float32) * 0.1,
        'gm_ln_g': 1.0 + 0.01 * nrm(ks[10], (DEPTH, GM_WIDTH), jnp.float32),
        'gm_ws': nrm(ks[11], (DEPTH, GM_GROUPS, GM_CHUNK, GM_CHUNK), jnp.float32) * GM_CHUNK ** -0.5,
        'gm_bs': 1.0 + 0.02 * nrm(ks[12], (DEPTH, GM_GROUPS, GM_CHUNK), jnp.float32),
        'w_proj_a': nrm(ks[13], (DEPTH, NA_WIDTH, D_MODEL), jnp.float32) * NA_WIDTH ** -0.5,
        'w_proj_b': nrm(ks[14], (DEPTH, GM_WIDTH, D_MODEL), jnp.float32) * GM_WIDTH ** -0.5,
        'w_out': nrm(ks[15], (DEPTH, D_MODEL, D_MODEL), jnp.float32) * D_MODEL ** -0.5,
        'peer_wq': nrm(ks[16], (DEPTH, D_MODEL, PEER_HEADS * PEER_QDIM), jnp.float32) * D_MODEL ** -0.5,
        'peer_keys': nrm(ks[17], (DEPTH, PEER_HEADS, 2, PEER_N_KEYS, PEER_HALF), jnp.float32) * PEER_HALF ** -0.5,
        'peer_u': nrm(ks[18], (DEPTH, PEER_EXPERTS, D_MODEL), jnp.float32) * D_MODEL ** -0.5,
        'peer_v': nrm(ks[19], (DEPTH, PEER_EXPERTS, D_MODEL), jnp.float32) * 0.5,
        'final_g': 1.0 + 0.01 * nrm(ks[20], (D_MODEL,), jnp.float32),
    }

def first_block(x, c, ctx, c_ctx, ada_w, ada_b, norm1_g, norm2_g, w_in, na_rpb, gm_ln_g, gm_ws, gm_bs,
              w_proj_a, w_proj_b, w_out, peer_wq, peer_keys, peer_u, peer_v, final_g):
    for layer in range(DEPTH):
        last = layer == DEPTH - 1
        sh1, sc1, g1, sh2, sc2, g2 = jnp.split(
            (jax.nn.silu(c) @ ada_w[layer] + ada_b[layer])[:, None, :], ADA_CHUNKS, axis=-1)
        csh1, csc1, cg1, csh2, csc2, cg2 = jnp.split(
            jax.nn.silu(c_ctx) @ ada_w[layer] + ada_b[layer], ADA_CHUNKS, axis=-1)
        w = w_in[layer]
        h = modulate(rmsnorm(x, norm1_g[layer]), sh1, sc1)
        hc = modulate(rmsnorm(ctx, norm1_g[layer]), csh1, csc1)
        q, k, v, gu, gv, ga, gb = jnp.split(h @ w, IN_SPLITS, axis=-1)
        if last:
            k_c, v_c = jnp.split(hc @ w[:, NA_WIDTH:3 * NA_WIDTH], 2, axis=-1)
        else:
            qc, k_c, v_c, guc, gvc, gac, gbc = jnp.split(hc @ w, IN_SPLITS, axis=-1)
        y_a = neighborhood_attention(heads(q), heads(k), heads(v), heads(k_c), heads(v_c), na_rpb[layer])
        y_b = spatial_gating(gu, gv, gm_ln_g[layer], gm_ws[layer], gm_bs[layer])
        x = x + g1 * merge_branches(y_a, y_b, ga, gb, w_proj_a[layer], w_proj_b[layer], w_out[layer])
        h2 = modulate(rmsnorm(x, norm2_g[layer]), sh2, sc2)
        x = x + g2 * peer_ffn(h2, peer_wq[layer], peer_keys[layer], peer_u[layer], peer_v[layer])
        if not last:
            yc_a = context_attention(heads(qc), heads(k_c), heads(v_c))
            yc_b = spatial_gating(guc, gvc, gm_ln_g[layer], gm_ws[layer], gm_bs[layer])
            ctx = ctx + cg1 * merge_branches(yc_a, yc_b, gac, gbc, w_proj_a[layer], w_proj_b[layer], w_out[layer])
            hc2 = modulate(rmsnorm(ctx, norm2_g[layer]), csh2, csc2)
            ctx = ctx + cg2 * peer_ffn(hc2, peer_wq[layer], peer_keys[layer], peer_u[layer], peer_v[layer])
    return rmsnorm(x, final_g)


ATT_HEADS = 8
ATT_KV_HEADS = 2
ATT_HEAD_DIM = 64
ATT_GROUP = ATT_HEADS // ATT_KV_HEADS
WINDOW = 128
ATT_BLOCK = 128
RET_HEADS = 4
RET_KEY_DIM = 128
RET_VAL_DIM = 256
RET_CHUNK = 128
D_FF = -(-8 * D_MODEL // (3 * 256)) * 256

ATT_Q_W = ATT_HEADS * ATT_HEAD_DIM
ATT_KV_W = ATT_KV_HEADS * ATT_HEAD_DIM
RET_QK_W = RET_HEADS * RET_KEY_DIM
RET_V_W = RET_HEADS * RET_VAL_DIM
IN_WIDTHS = (ATT_Q_W, ATT_KV_W, ATT_KV_W, RET_QK_W, RET_QK_W, RET_V_W, RET_V_W, D_MODEL, D_MODEL)
D_IN = sum(IN_WIDTHS)


def rms_norm(x, g):
    xf = x.astype(jnp.float32)
    y = xf * lax.rsqrt(jnp.mean(xf * xf, axis=-1, keepdims=True) + EPS) * g.astype(jnp.float32)
    return y.astype(x.dtype)

def alibi_slopes(n_heads):
    return jnp.exp2(-8.0 * (jnp.arange(n_heads, dtype=jnp.float32) + 1.0) / n_heads)

def sliding_window_attention(q, k, v, sinks):
    b, s, _, hd = q.shape
    nb = s // ATT_BLOCK
    f32 = jnp.float32
    qb = q.astype(f32).reshape(b, nb, ATT_BLOCK, ATT_KV_HEADS, ATT_GROUP, hd) * (hd ** -0.5)

    def band(t):
        tp = jnp.pad(t.astype(f32), ((0, 0), (ATT_BLOCK, 0), (0, 0), (0, 0)))
        prev = tp[:, :s].reshape(b, nb, ATT_BLOCK, ATT_KV_HEADS, hd)
        cur = tp[:, ATT_BLOCK:].reshape(b, nb, ATT_BLOCK, ATT_KV_HEADS, hd)
        return jnp.concatenate([prev, cur], axis=2)

    kb, vb = band(k), band(v)
    i = jnp.arange(ATT_BLOCK)[:, None]
    j = jnp.arange(2 * ATT_BLOCK)[None, :]
    dist = i + ATT_BLOCK - j
    key_pos = jnp.arange(nb)[:, None, None] * ATT_BLOCK - ATT_BLOCK + j[None]
    valid = (dist >= 0) & (dist < WINDOW) & (key_pos >= 0)
    slopes = alibi_slopes(ATT_HEADS).reshape(ATT_KV_HEADS, ATT_GROUP)
    scores = jnp.einsum('bnikgd,bnjkd->bnkgij', qb, kb) - slopes[:, :, None, None] * dist.astype(f32)
    scores = jnp.where(valid[None, :, None, None], scores, -jnp.inf)
    sink = jnp.broadcast_to(sinks.astype(f32).reshape(ATT_KV_HEADS, ATT_GROUP)[None, None, :, :, None, None],
                            scores.shape[:-1] + (1,))
    probs = jax.nn.softmax(jnp.concatenate([scores, sink], axis=-1), axis=-1)[..., :-1]
    out = jnp.einsum('bnkgij,bnjkd->bnikgd', probs, vb)
    return out.reshape(b, s, ATT_Q_W)

def retention_chunkwise(q, k, v):
    b, s, h, dk = q.shape
    dv = v.shape[-1]
    nc = s // RET_CHUNK
    f32 = jnp.float32
    log_g = jnp.log(1.0 - jnp.exp2(-5.0 - jnp.arange(h, dtype=f32)))
    idx = jnp.arange(RET_CHUNK, dtype=f32)
    diff = idx[:, None] - idx[None, :]
    decay_intra = jnp.where(diff >= 0, jnp.exp(log_g[:, None, None] * jnp.maximum(diff, 0.0)), 0.0)
    decay_q = jnp.exp(log_g[:, None] * (idx + 1.0)).T[None, :, :, None]
    decay_k = jnp.exp(log_g[:, None] * (RET_CHUNK - 1.0 - idx)).T[None, :, :, None]
    decay_chunk = jnp.exp(log_g * RET_CHUNK)[None, :, None, None]

    def to_chunks(t):
        return t.astype(f32).reshape(b, nc, RET_CHUNK, h, t.shape[-1]).transpose(1, 0, 2, 3, 4)

    qc, kc, vc = to_chunks(q), to_chunks(k * (dk ** -0.5)), to_chunks(v)

    def step(state, inp):
        qi, ki, vi = inp
        scores = jnp.einsum('bihd,bjhd->bhij', qi, ki) * decay_intra
        o = jnp.einsum('bhij,bjhv->bihv', scores, vi)
        o = o + jnp.einsum('bihd,bhdv->bihv', qi, state) * decay_q
        state = decay_chunk * state + jnp.einsum('bjhd,bjhv->bhdv', ki * decay_k, vi)
        return state, o

    state0 = jnp.zeros((b, h, dk, dv), f32)
    _, o = lax.scan(step, state0, (qc, kc, vc))
    return o.transpose(1, 0, 2, 3, 4).reshape(b, s, h, dv)

def head_group_norm(o, gain):
    b, s, h, dv = o.shape
    mu = jnp.mean(o, axis=-1, keepdims=True)
    var = jnp.mean(jnp.square(o - mu), axis=-1, keepdims=True)
    return ((o - mu) * lax.rsqrt(var + EPS)).reshape(b, s, h * dv) * gain.astype(jnp.float32)

def second_inputs(seed: int = 0) -> dict:
    key = jax.random.key(seed)
    ks = jax.random.split(key, 16)
    f32 = jnp.float32

    def w(k, shape, fan_in):
        return jax.random.normal(k, shape, f32) * (fan_in ** -0.5)

    return {
        "x": jax.random.normal(ks[0], (BATCH, SEQ, D_MODEL), f32),
        "norm_mix": 1.0 + 0.02 * jax.random.normal(ks[1], (DEPTH, D_MODEL), f32),
        "w_in": w(ks[2], (DEPTH, D_MODEL, D_IN), D_MODEL),
        "att_sinks": 0.5 * jax.random.normal(ks[3], (DEPTH, ATT_HEADS), f32),
        "ret_gn_gain": 1.0 + 0.02 * jax.random.normal(ks[4], (DEPTH, RET_V_W), f32),
        "w_att_o": w(ks[5], (DEPTH, ATT_Q_W, D_MODEL), ATT_Q_W),
        "w_ret_o": w(ks[6], (DEPTH, RET_V_W, D_MODEL), RET_V_W),
        "w_out": w(ks[7], (DEPTH, D_MODEL, D_MODEL), D_MODEL),
        "norm_ffn": 1.0 + 0.02 * jax.random.normal(ks[8], (DEPTH, D_MODEL), f32),
        "w_gate": w(ks[9], (DEPTH, D_MODEL, D_FF), D_MODEL),
        "w_up": w(ks[10], (DEPTH, D_MODEL, D_FF), D_MODEL),
        "w_down": w(ks[11], (DEPTH, D_FF, D_MODEL), D_FF),
        "final_norm": 1.0 + 0.02 * jax.random.normal(ks[12], (D_MODEL,), f32),
    }

def second_block(x, norm_mix, w_in, att_sinks, ret_gn_gain, w_att_o, w_ret_o, w_out,
              norm_ffn, w_gate, w_up, w_down, final_norm):
    b, s, _ = x.shape
    offsets = [int(o) for o in np.cumsum(IN_WIDTHS)[:-1]]
    for l in range(DEPTH):
        h = rms_norm(x, norm_mix[l])
        proj = h @ w_in[l]
        aq, ak, av, rq, rk, rv, rg, ga, gr = jnp.split(proj, offsets, axis=-1)
        att = sliding_window_attention(
            aq.reshape(b, s, ATT_HEADS, ATT_HEAD_DIM),
            ak.reshape(b, s, ATT_KV_HEADS, ATT_HEAD_DIM),
            av.reshape(b, s, ATT_KV_HEADS, ATT_HEAD_DIM),
            att_sinks[l]).astype(x.dtype)
        ret = retention_chunkwise(
            rq.reshape(b, s, RET_HEADS, RET_KEY_DIM),
            rk.reshape(b, s, RET_HEADS, RET_KEY_DIM),
            rv.reshape(b, s, RET_HEADS, RET_VAL_DIM))
        ret = head_group_norm(ret, ret_gn_gain[l]).astype(x.dtype) * jax.nn.silu(rg)
        merged = jax.nn.sigmoid(ga) * (att @ w_att_o[l]) + jax.nn.sigmoid(gr) * (ret @ w_ret_o[l])
        x = x + merged @ w_out[l]
        h = rms_norm(x, norm_ffn[l])
        x = x + (jax.nn.silu(h @ w_gate[l]) * (h @ w_up[l])) @ w_down[l]
    return rms_norm(x, final_norm)


def setup_inputs(seed=0):
    out = dict(first_inputs(seed))
    for name, value in second_inputs(seed + 1).items():
        if name != "x":
            out[name + "_2"] = value
    return out


def reference(
    x, c, ctx, c_ctx, ada_w, ada_b, norm1_g, norm2_g, w_in, na_rpb, gm_ln_g, gm_ws, gm_bs,
    w_proj_a, w_proj_b, w_out, peer_wq, peer_keys, peer_u, peer_v, final_g, norm_mix_2, w_in_2,
    att_sinks_2, ret_gn_gain_2, w_att_o_2, w_ret_o_2, w_out_2, norm_ffn_2, w_gate_2, w_up_2,
    w_down_2, final_norm_2,
):
    x = first_block(
        x, c, ctx, c_ctx, ada_w, ada_b, norm1_g, norm2_g, w_in, na_rpb, gm_ln_g, gm_ws, gm_bs,
        w_proj_a, w_proj_b, w_out, peer_wq, peer_keys, peer_u, peer_v, final_g,
    )
    return second_block(
        x, norm_mix_2, w_in_2, att_sinks_2, ret_gn_gain_2, w_att_o_2, w_ret_o_2, w_out_2,
        norm_ffn_2, w_gate_2, w_up_2, w_down_2, final_norm_2,
    )


_drawn_inputs = setup_inputs


def setup_inputs(seed=0):
    import zlib

    import numpy as np

    out = dict(_drawn_inputs(seed))
    spreads = {}
    factors = {'ctx': 4.958,
     'c_ctx': 3.24,
     'ada_b': 2.836,
     'norm1_g': 8.0,
     'norm2_g': 41.071,
     'na_rpb': 36.061,
     'gm_ln_g': 23.683,
     'gm_bs': 8.0,
     'final_g': 4.511,
     'norm_mix_2': 3.615,
     'att_sinks_2': 64.0,
     'ret_gn_gain_2': 8.0,
     'norm_ffn_2': 12.054,
     'final_norm_2': 8.012}
    for name, (base, spread) in spreads.items():
        noise = np.random.default_rng([zlib.crc32(name.encode()), seed]).standard_normal(out[name].shape)
        drawn = base * np.exp(spread * noise) if base else spread * noise
        out[name] = __import__('jax').numpy.asarray(drawn.astype(out[name].dtype))
    for name, factor in factors.items():
        out[name] = (out[name] * factor).astype(out[name].dtype)
    return out
```

```python
from contextlib import ExitStack

import concourse.bass as bass
from concourse import mybir

F32 = mybir.dt.float32
FR = mybir.dt.float32r
U32 = mybir.dt.uint32
ALU = mybir.AluOpType
ACT = mybir.ActivationFunctionType
AX_X = mybir.AxisListType.X

P = 128
D = 1024
KB = D // P
S = 512
TB = S // P
CTX = 256
R = 4
EPS = 1e-6
NEG = -1e30
HD = 64
NH = 8
SCALE = HD ** -0.5
DFF = 2816
FB = DFF // P
WIN = 14 * 64

PARTS = [("q", 4), ("k", 4), ("v", 4), ("gu", 4), ("gv", 4), ("gates", 16), ("pa", 4), ("pb", 4), ("out", 8),
         ("wq", 16), ("U", 128), ("V", 128), ("aq", 4), ("rq", 4), ("rk", 4), ("rv", 8), ("av", 1), ("ak", 1),
         ("rg", 8), ("ga2", 8), ("atto", 4), ("gr2", 8), ("reto", 8), ("out2", 8), ("gateup", 2 * FB), ("down", FB)]
G0 = {}
NT = 0
for _name, _n in PARTS:
    G0[_name] = NT
    NT += _n
COUNT = dict(PARTS)
K_FORM = {"V", "down"}

COLS = {}
_c = 0
for _name, _n in [("n1", 8), ("n2", 8), ("fin1", 8), ("mix2", 8), ("ffn2", 8), ("fin2", 8), ("adab", 48), ("lng", 4),
                  ("gn", 8), ("sink", 8), ("slope", 8)]:
    COLS[_name] = (_c, _c + _n)
    _c += _n
NCOL = _c

U_LEAD = 3
U_GATE = 16
U_TAIL = 32 - TB * U_LEAD - U_GATE
CONST0 = 64
MASKED = -3e38


class Tally:

    def __init__(self, start=0):
        self.n, self.reg, self.per = start, None, 0

    def add(self, k=1):
        self.n += k
        return self

    def at(self, back=0):
        return self.n - back if self.reg is None else self.reg * self.per + (self.n - back)

    def enter(self, reg, per):
        self.reg, self.per, self.first = reg, per, self.n

    def leave(self, times):
        assert self.n - self.first == self.per, (self.n - self.first, self.per)
        self.n, self.reg = self.first + self.per * times, None


def chain_loop(eng, tally, times, per, body):
    with eng.Fori(0, times) as i:
        tally.enter(i, per)
        body(i)
        tally.leave(times)


def build(nc, A, out):
    with ExitStack() as ctx:
        def sem(name):
            return ctx.enter_context(nc.semaphore(name))

        def allocator(stack):
            return lambda name, shape, dt=F32: stack.enter_context(nc.sbuf_tensor(name, shape, dt))

        sb = allocator(ctx)
        wraw = sb("wraw", [P, R, KB, P])
        whi = sb("whi", [P, R, KB, P], FR)
        wlo = sb("wlo", [P, R, KB, P], FR)
        X = sb("X", [P, KB, S])
        HH = sb("HH", [P, KB, S], FR)
        HL = sb("HL", [P, KB, S], FR)
        T = sb("T", [P, KB, S])
        cols = sb("cols", [P, NCOL])
        mod = sb("mod", [P, 48, 2])
        gsc = sb("gsc", [P, 3, KB])
        ident = sb("ident", [P, P])
        ones = sb("ones", [P, P])
        iota = sb("iota", [P, P])
        eps = sb("eps", [P, 1])
        rms = sb("rms", [P, S])
        rstd = sb("rstd", [P, S])
        st = sb("st", [P, 24])
        bn = sb("bn", [P, TB, 6])

        m1 = ExitStack()
        a1 = allocator(m1)
        adaw = a1("adaw", [P, R, KB, P])
        YAH = a1("YAH", [P, 4, S], FR)
        YAL = a1("YAL", [P, 4, S], FR)
        s2 = ExitStack()
        a2 = allocator(s2)
        QT = a2("QT", [P, 4, S])
        KT = a2("KT", [P, 4, S + CTX])
        VV = a2("VV", [P, 6, S])
        s3 = ExitStack()
        a3 = allocator(s3)
        CX = a3("CX", [P, KB, CTX])
        CH = a3("CH", [P, KB, CTX], FR)
        CL = a3("CL", [P, KB, CTX], FR)
        cc = a3("cc", [P, KB, 2])
        scc = a3("scc", [P, KB, 2])
        s3.close()
        s3 = ExitStack()
        a3 = allocator(s3)
        E = a3("E", [P, 2, 2, WIN])
        PT = a3("PT", [P, 2, 6, P])
        wmask = a3("wmask", [P, HD])
        mx = a3("mx", [P, 3, 3])
        s3.close()
        s2.close()
        SS = T[:, :, :].rearrange("p a b -> p (a b)")[:, 0:2304].rearrange("p (u n) -> p u n", u=3)
        s2 = ExitStack()
        a2 = allocator(s2)
        SG = a2("SG", [P, 16, S])
        YBH = a2("YBH", [P, 4, S], FR)
        YBL = a2("YBL", [P, 4, S], FR)
        wsT = a2("wsT", [P, NH, P])
        bsb = a2("bsb", [P, 4, P])
        s2.close()
        UT = T[:, 0:4, :]
        GV = T[:, 4:8, :]
        MX = T[:, 4:8, :]
        m1.close()

        m1 = ExitStack()
        a1 = allocator(m1)
        GS = a1("GS", [P, 2, P, 64])
        actb = a1("actb", [P, 2, S])
        IT = a1("IT", [P, 3, S])
        GH = a1("GH", [P, S], FR)
        s2 = ExitStack()
        a2 = allocator(s2)
        small = a2("small", [P, 16, 16])
        tki = a2("tki", [P, 16, 16], U32)
        tkf = a2("tkf", [P, 16, 16])
        bv = a2("bv", [P, NH, 16])
        bp = a2("bp", [P, NH, 16], U32)
        bab = a2("bab", [P, 2, NH, 16], U32)
        babf = a2("babf", [P, 2, NH, 16])
        sel3 = a2("sel3", [P, 3, P])
        hs = a2("hs", [P, 2, NH])
        s2.close()
        s2 = ExitStack()
        a2 = allocator(s2)
        A1 = a2("A1", [P, 8, P], FR)
        A2 = a2("A2", [P, 8, P], FR)
        B1 = a2("B1", [P, 8, P], FR)
        s2.close()
        m1.close()
        QP = GS[:, 0, :, :].rearrange("p a b -> p (a b)").rearrange("p (n t) -> p n t", t=S)
        SC = GS[:, 1, :, :].rearrange("p a b -> p (a b)").rearrange("p (b n k) -> p b n k", b=TB, n=16)
        keysT = T[:, 0:4, :].rearrange("p a b -> p (a b)").rearrange("p (n k) -> p n k", k=P)
        cand = T[:, 0:4, :].rearrange("p a b -> p (a b)").rearrange("p (h a b) -> p h a b", h=NH, a=16)
        SSc = T[:, 4:8, :].rearrange("p a b -> p (a b)").rearrange("p (n k) -> p n k", k=P)
        m1 = ExitStack()
        a1 = allocator(m1)
        AJ = a1("AJ", [P, R, S])
        GJ = a1("GJ", [P, R, 8, 64])
        WH = a1("WH", [P, R, S], FR)
        WL = a1("WL", [P, R, S], FR)
        m1.close()

        m1 = ExitStack()
        a1 = allocator(m1)
        ATH = a1("ATH", [P, 4, S], FR)
        ATL = a1("ATL", [P, 4, S], FR)
        OT = a1("OT", [P, 8, S])
        s2 = ExitStack()
        a2 = allocator(s2)
        AQ = a2("AQ", [P, 4, S])
        RQ = a2("RQ", [P, 4, S])
        RK = a2("RK", [P, 4, S])
        RV = a2("RV", [P, 4, D])
        AK = a2("AK", [P, S])
        AV = a2("AV", [P, 4, P])
        s2.close()
        flat = T[:, :, :].rearrange("p a b -> p (a b)")
        AS = flat[:, 768:1536].rearrange("p (u n) -> p u n", u=3)
        APT = flat[:, 1536:2048].rearrange("p (u k q) -> p u k q", u=2, k=2)
        alibi = flat[:, 2048:2304]
        amx = flat[:, 2304:2328].rearrange("p (u c) -> p u c", u=3)
        RSC = T[:, 5:7, :]
        DEC = T[:, 7, :]
        s2 = ExitStack()
        a2 = allocator(s2)
        RH = a2("RH", [P, 8, S], FR)
        RL = a2("RL", [P, 8, S], FR)
        rst4 = a2("rst4", [P, 4, S])
        s2.close()
        m1.close()
        hid = ExitStack()
        a1 = allocator(hid)
        FH = a1("FH", [P, FB, S], FR)
        FL = a1("FL", [P, FB, S], FR)
        hid.close()
        bank = [ctx.enter_context(nc.psum_tensor(f"bank{b}", [P, S], F32)) for b in range(8)]

        act_dram = nc.dram_tensor("act_dram", (P, P, S), F32).ap()
        gate_dram = nc.dram_tensor("gate_dram", (8, P, P, 64), F32).ap()

        w_in = [sem(f"w_in{s}") for s in range(R)]
        w_hi = sem("w_hi")
        w_lo = sem("w_lo")
        tile_done = sem("tile_done")
        tile_evac = sem("tile_evac")
        ada_in = [sem(f"ada_in{s}") for s in range(R)]
        ada_used = sem("ada_used")
        ada_evac = sem("ada_evac")
        const_in = sem("const_in")
        const2_in = sem("const2_in")
        n_eps = sem("n_eps")
        r_pv = sem("r_pv")
        ctx_in = sem("ctx_in")
        late_in = sem("late_in")
        keys_in = sem("keys_in")
        alibi_in = sem("alibi_in")
        dec_in = sem("dec_in")
        bias_in = [sem(f"bias_in{b}") for b in range(2)]
        silu_c = sem("silu_c")
        n_sq = sem("n_sq")
        n_sum = sem("n_sum")
        n_root = sem("n_root")
        n_scaled = sem("n_scaled")
        n_aff = sem("n_aff")
        n_hi = sem("n_hi")
        n_lo = sem("n_lo")
        res_done = sem("res_done")
        gsc_ready = sem("gsc_ready")
        dve = sem("dve_chain")
        at_s = sem("at_s")
        at_masked = sem("at_masked")
        at_exp = sem("at_exp")
        at_p = sem("at_p")
        at_t = sem("at_t")
        at_pt = sem("at_pt")
        at_av = sem("at_av")
        at_hi = sem("at_hi")
        at_lo = sem("at_lo")
        gm_root = sem("gm_root")
        gm_var = sem("gm_var")
        gm_vn = sem("gm_vn")
        gm_mix = sem("gm_mix")
        gm_y = sem("gm_y")
        gm_hi = sem("gm_hi")
        gm_lo = sem("gm_lo")
        mg_m = sem("mg_m")
        mg_hi = sem("mg_hi")
        mg_lo = sem("mg_lo")
        sc_done = sem("sc_done")
        sc_evac = sem("sc_evac")
        tk_diff = sem("tk_diff")
        tk_exp = sem("tk_exp")
        tk_sel = sem("tk_sel")
        tk_tr = sem("tk_tr")
        tk_it = sem("tk_it")
        tk_gate = sem("tk_gate")
        oh_ready = sem("oh_ready")
        g_done = sem("g_done")
        g_evac = sem("g_evac")
        g_out = [sem(f"g_out{b}") for b in range(2)]
        act_out = [sem(f"act_out{b}") for b in range(2)]
        ag_in = [sem(f"ag_in{s}") for s in range(R)]
        pw = sem("pw")
        pw_hi = sem("pw_hi")
        pw_lo = sem("pw_lo")
        r_s = sem("r_s")
        r_sd = sem("r_sd")
        r_oc = sem("r_oc")
        gn_mu = sem("gn_mu")
        gn_cen = sem("gn_cen")
        gn_sq = sem("gn_sq")
        gn_var = sem("gn_var")
        gn_root = sem("gn_root")
        gn_done = sem("gn_done")
        rg_mul = sem("rg_mul")
        rg_hi = sem("rg_hi")
        rg_lo = sem("rg_lo")
        ff_mul = sem("ff_mul")
        ff_lo = sem("ff_lo")
        out_rdy = sem("out_rdy")
        out_done = sem("out_done")

        def col(name, k, rows=slice(0, P)):
            a, b = COLS[name]
            return cols[rows, a + k:a + k + 1]

        def bc(ap, axis, n):
            dims = [list(x) for x in ap.ap]
            dims.insert(axis, [0, n])
            return bass.AP(tensor=ap.tensor, offset=ap.offset, ap=dims)

        def evac_before(g):
            return g if g <= G0["V"] else g - COUNT["V"]

        block = ctx.enter_context(nc.Block())

        @block.sync
        def _(sp):
            NCONST = 0
            for dst, src in ((X[:, :, :], A["x"]), (cols[:, :], A["cols"]), (ones[:, :], A["ones"]),
                             (cc[:, :, :], A["c"])):
                sp.dma_start(dst, src).then_inc(const_in, 16)
                NCONST += 16
            assert NCONST == CONST0

            def load_ada(a, slot, peeled=False):
                if not peeled:
                    sp.wait_ge(ada_used, a - R + 1)
                sp.dma_start(adaw[:, slot, :, :].rearrange("p k c -> p (k c)"), A["ada"][a, :, :])\
                    .then_inc(ada_in[slot], 16)

            def load_w(g, slot, peeled=False):
                if not peeled:
                    sp.wait_ge(w_lo, g - R + 1)
                sp.dma_start(wraw[:, slot, :, :].rearrange("p k c -> p (k c)"), A["w"][g, :, :])\
                    .then_inc(w_in[slot], 16)

            for a in range(R):
                load_ada(a, a, peeled=True)
            sp.dma_start(CX[:, :, :], A["ctx"]).then_inc(ctx_in, 16)
            for dst, src in ((ident[:, :], A["ident"]), (iota[:, :], A["iota"])):
                sp.dma_start(dst, src).then_inc(const2_in, 16)
            for g in range(R):
                load_w(g, g, peeled=True)
            with sp.Fori(0, 3) as i:
                for u in range(4):
                    load_ada(i * 4 + (4 + u), u)
            with sp.Fori(0, 4) as i:
                for u in range(4):
                    load_w(i * 4 + (4 + u), u)
            with sp.Fori(0, 4) as i:
                for u in range(4):
                    load_w(i * 4 + (G0["gates"] + u), u)
                    for k in range(2):
                        load_ada(i * 8 + (16 + 2 * u + k), (2 * u + k) % R)
            n = (G0["U"] - G0["pa"]) // 4 + TB * U_LEAD
            with sp.Fori(0, n) as i:
                for u in range(4):
                    load_w(i * 4 + (G0["pa"] + u), u)
            gu0 = G0["U"] + 4 * TB * U_LEAD

            def store_g(b, buf):
                sp.wait_ge(g_evac, b * 16 + 16)
                sp.dma_start(gate_dram[b, :, :, :].rearrange("i j t -> i (j t)"),
                             GS[:, buf, :, :].rearrange("p j t -> p (j t)")).then_inc(g_out[buf], 16)

            for u in range(8):
                load_w(gu0 + u, u % R)
            for u in range(4):
                load_w(gu0 + 8 + u, u % R)
            store_g(0, 0)
            for u in range(4):
                load_w(gu0 + 12 + u, u % R)
            with sp.Fori(0, 3) as i:
                for half in range(2):
                    for u in range(4):
                        load_w(i * 16 + (gu0 + 16 + 8 * half + u), u)
                    store_g(i * 2 + (1 + half), (1 + half) % 2)
                    for u in range(4):
                        load_w(i * 16 + (gu0 + 20 + 8 * half + u), u)
            gt0 = gu0 + 4 * U_GATE
            for u in range(4):
                load_w(gt0 + u, u)
            store_g(7, 1)
            with sp.Fori(0, U_TAIL - 1) as i:
                for u in range(4):
                    load_w(i * 4 + (gt0 + 4 + u), u)

            def load_ag(j, slot, peeled=False):
                if not peeled:
                    sp.wait_ge(pw_lo, j - R + 1)
                sp.dma_start(AJ[:, slot, :], act_dram[j, :, :]).then_inc(ag_in[slot], 16)
                sp.dma_start(GJ[:, slot, :, :], gate_dram[:, :, j, :].rearrange("b i t -> i b t"))\
                    .then_inc(ag_in[slot], 16)

            for b in range(2):
                sp.wait_ge(g_out[b], 64)
            for u in range(R):
                sp.wait_ge(act_out[u % 2], 16 * (u // 2 + 1))
                load_ag(u, u, peeled=True)
            for u in range(R):
                load_w(G0["V"] + u, u)
            for b in range(2):
                sp.wait_ge(act_out[b], 16 * 64)
            with sp.Fori(0, 31) as i:
                for u in range(R):
                    load_w(i * 4 + (G0["V"] + 4 + u), u)
                    load_ag(i * 4 + (4 + u), u)
            n = (NT - G0["aq"]) // 4
            with sp.Fori(0, n) as i:
                for u in range(4):
                    load_w(i * 4 + (G0["aq"] + u), u)
            for kb in range(KB):
                sp.wait_ge(out_rdy, kb + 1)
                sp.dma_start(out[:, kb, :], T[:, kb, :]).then_inc(out_done, 16)
            sp.wait_ge(out_done, 16 * KB)

        @block.gpsimd
        def _(pool):
            def lo(g, slot):
                pool.wait_ge(w_hi, g + 1)
                nc.gpsimd.tensor_tensor(wlo[:, slot, :, :].rearrange("p k c -> p (k c)"),
                                        wraw[:, slot, :, :].rearrange("p k c -> p (k c)"),
                                        whi[:, slot, :, :].rearrange("p k c -> p (k c)").bitcast(F32),
                                        ALU.subtract).then_inc(w_lo, 1)

            def los(g0, n):
                while n and g0 % R:
                    lo(g0, g0 % R)
                    g0, n = g0 + 1, n - 1
                if n >= 8:
                    with pool.Fori(0, n // 4) as i:
                        for u in range(4):
                            lo(i * 4 + (g0 + u), u)
                    g0, n = g0 + n // 4 * 4, n % 4
                for u in range(n):
                    lo(g0 + u, (g0 + u) % R)

            los(0, 15)
            for pair in range(4):
                b = pair % 2
                if pair == 0:
                    pool.wait_ge(tile_evac, G0["gu"])
                    pool.wait_ge(n_lo, 2 * KB)
                if pair >= 2:
                    pool.wait_ge(at_masked, 8 * (pair - 1))
                for hh in range(2):
                    for r in range(2):
                        L = 15 * 127
                        skewed = bass.AP(tensor=A["rpb"].tensor, offset=(2 * pair + hh) * L + (1 - r) * 127 + 63,
                                         ap=[[8 * L - 1, 64], [127, 14], [1, 64]])
                        pool.dma_start(E[64 * r:64 * r + 64, b, hh, :].rearrange("p (m k) -> p m k", k=64), skewed)\
                            .then_inc(bias_in[b], 16)
                if pair == 0:
                    pool.dma_start(wmask[:, :], A["wmask"]).then_inc(late_in, 16)
            los(15, G0["gates"] - 15)
            pool.wait_ge(at_lo, 32)
            pool.dma_start(wsT[:, :, :], A["wsT"]).then_inc(late_in, 16)
            pool.dma_start(bsb[:, :, :], A["bs"]).then_inc(late_in, 16)
            los(G0["gates"], G0["wq"] - G0["gates"] + 3)
            pool.wait_ge(n_lo, 3 * KB)
            pool.dma_start(keysT, A["keys"]).then_inc(keys_in, 16)
            los(G0["wq"] + 3, 17)
            los(G0["U"] + 4, G0["rg"] + 3 - (G0["U"] + 4))
            pool.wait_ge(tile_evac, evac_before(G0["rg"]))
            pool.dma_start(alibi, A["alibi"]).then_inc(alibi_in, 16)
            for h in range(4):
                if h:
                    pool.wait_ge(r_sd, 4 * h)
                pool.dma_start(DEC, A["dec"][h, :, :]).then_inc(dec_in, 16)
            los(G0["rg"] + 3, NT - G0["rg"] - 3)

        @block.scalar
        def _(act):
            def hi(g, slot, turns, peeled=False):
                act.wait_ge(w_in[slot], turns)
                if not peeled:
                    act.wait_ge(tile_done, g - R + 1)
                nc.scalar.activation(whi[:, slot, :, :].rearrange("p k c -> p (k c)"),
                                     wraw[:, slot, :, :].rearrange("p k c -> p (k c)"), ACT.Copy).then_inc(w_hi, 1)

            def ahead(g0, u, i=None):
                t = g0 + u + 3
                if i is None:
                    if t < NT:
                        hi(t, t % R, 16 * (t // R + 1), peeled=t < R)
                else:
                    hi(i * 4 + t, t % R, i * 16 + 16 * (t // R + 1))

            def tile_ready(g):
                act.wait_ge(tile_done, g + 1)

            norms = [0]
            done_blocks = [0]

            def norm_squares(src, width, ready=None, block_ready=None):
                for kb in range(KB):
                    if kb == 0 and ready:
                        for s_, v_ in ready:
                            act.wait_ge(s_, v_)
                    if block_ready:
                        act.wait_ge(block_ready[0], block_ready[1] + kb + 1)
                    nc.scalar.activation(T[:, kb, 0:width], src[:, kb, :], ACT.Square).then_inc(n_sq, 1)

            def norm_root(width, b=4):
                norms[0] += 1
                act.wait_ge(n_sum, norms[0])
                nc.scalar.activation(rms[:, 0:width], bank[b][:, 0:width], ACT.Sqrt, bias=eps[:, 0:1], scale=1.0 / D)\
                    .then_inc(n_root, 1)

            def norm_apply(width, gain, shift, H):
                for kb in range(KB):
                    done_blocks[0] += 1
                    act.wait_ge(n_scaled, done_blocks[0])
                    kw = {} if shift is None else {"bias": shift(kb)}
                    nc.scalar.activation(T[:, kb, 0:width], T[:, kb, 0:width], ACT.Identity, scale=gain(kb), **kw)\
                        .then_inc(n_aff, 1)
                    act.wait_ge(n_aff, done_blocks[0])
                    nc.scalar.activation(H[:, kb, :], T[:, kb, 0:width], ACT.Copy).then_inc(n_hi, 1)

            act.wait_ge(const_in, CONST0)
            nc.scalar.activation(scc[:, :, :], cc[:, :, :], ACT.Silu).then_inc(silu_c, 1)
            norm_squares(X, S)
            act.wait_ge(n_eps, 1)
            norm_root(S)
            for g in range(3):
                ahead(-3, g)
            act.wait_ge(gsc_ready, 1)
            norm_apply(S, lambda kb: gsc[:, 0, kb:kb + 1], lambda kb: mod[:, kb, 0:1], HH)
            norm_squares(CX, CTX, ready=[(n_lo, KB), (ctx_in, 16)])
            norm_root(CTX)
            norm_apply(CTX, lambda kb: gsc[:, 1, kb:kb + 1], lambda kb: mod[:, kb, 1:2], CH)
            for g in range(12):
                ahead(g, 0)

            def at1_evac(n, it):
                act.wait_ge(at_t, it * 16 + (n + 1))
                if n >= 2:
                    act.wait_ge(at_av, it * 16 + (n - 1))
                b = n % 2
                nc.scalar.activation(PT[:, b, 0:4, :].rearrange("p k q -> p (k q)"), bank[2 * b][:, :], ACT.Copy)\
                    .then_inc(at_pt, 1)
                nc.scalar.activation(PT[:, b, 4:6, :].rearrange("p k q -> p (k q)"), bank[2 * b + 1][:, 0:256],
                                     ACT.Copy).then_inc(at_pt, 1)

            def at1_hi(n, it):
                act.wait_ge(at_av, it * 16 + (n + 1))
                pair, hh, a = n // 8, n // 4 % 2, n % 4
                r = slice(64 * hh, 64 * hh + 64)
                nc.scalar.activation(YAH[r, bass.ds(it * 2 + pair, 1), a * P:(a + 1) * P]
                                     .rearrange("p o q -> p (o q)"),
                                     bank[2 * (n % 2) + 1][r, 256:384], ACT.Copy).then_inc(at_hi, 1)

            with act.Fori(0, 2) as it:
                for n in range(16 + 3):
                    if n < 16:
                        act.wait_ge(at_masked, it * 16 + (n + 1))
                        nc.scalar.activation(SS[:, n % 3, :], SS[:, n % 3, :], ACT.Exp, bias=mx[:, n % 3, 0:1],
                                             accum_out=mx[:, n % 3, 1:2]).then_inc(at_exp, 1)
                    if 2 <= n < 18:
                        at1_evac(n - 2, it)
                    if n >= 3:
                        at1_hi(n - 3, it)

            for u in range(4):
                ahead(G0["gu"], u)
                tile_ready(G0["gu"] + u)
                if u == 0:
                    act.wait_ge(at_lo, 32)
                nc.scalar.activation(UT[:, u, :], bank[u][:, :], ACT.Gelu_apprx_tanh).then_inc(tile_evac, 1)
            for u in range(4):
                ahead(G0["gv"], u)
            tile_ready(G0["gv"] + 3)
            for b in (3, 2, 1, 0):
                nc.scalar.activation(GV[:, b, :], bank[4 + b][:, :], ACT.Gelu_apprx_tanh).then_inc(tile_evac, 1)
            act.wait_ge(gm_var, 4)
            nc.scalar.activation(st[:, 8:12], st[:, 4:8], ACT.Sqrt, bias=eps[:, 0:1]).then_inc(gm_root, 1)
            with act.Fori(0, 4) as i:
                for u in range(4):
                    ahead(G0["gates"], u, i)
                    tile_ready(i * 4 + (G0["gates"] + u))
                    nc.scalar.activation(SG[:, bass.ds(i * 4 + u, 1), :].rearrange("p o t -> p (o t)"),
                                         bank[u][:, :], ACT.Sigmoid).then_inc(tile_evac, 1)
            for b in range(4):
                act.wait_ge(gm_y, b + 1)
                nc.scalar.activation(YBH[:, b, :], MX[:, b, :], ACT.Copy).then_inc(gm_hi, 1)
            for u in range(8):
                ahead(G0["pa"], u)
                if u >= 4:
                    for k in range(2):
                        kb = 2 * (u - 4) + k
                        act.wait_ge(mg_m, kb + 1)
                        nc.scalar.activation(HH[:, kb, :], T[:, kb, :], ACT.Copy).then_inc(mg_hi, 1)
            for u in range(8):
                ahead(G0["out"], u)
            norm_squares(X, S, ready=[(mg_lo, KB)], block_ready=(tile_evac, G0["out"]))
            norm_root(S)
            norm_apply(S, lambda kb: gsc[:, 2, kb:kb + 1], lambda kb: mod[:, 24 + kb, 0:1], HH)
            with act.Fori(0, 4) as i:
                for u in range(4):
                    ahead(G0["wq"], u, i)
                    tile_ready(i * 4 + (G0["wq"] + u))
                    nc.scalar.activation(QP[:, bass.ds(i * 4 + u, 1), :].rearrange("p o t -> p (o t)"),
                                         bank[u][:, :], ACT.Copy).then_inc(tile_evac, 1)
            for n in range(16):
                act.wait_ge(sc_done, n + 1)
                nc.scalar.activation(SC[:, n // 4, 4 * (n % 4):4 * (n % 4) + 4, :].rearrange("p n k -> p (n k)"),
                                     bank[4 + n % 4][:, :], ACT.Copy).then_inc(sc_evac, 1)

            def act_tile(j, u, evac_turns=None):
                tile_ready(j + G0["U"])
                if evac_turns is not None:
                    act.wait_ge(act_out[u % 2], evac_turns)
                nc.scalar.activation(actb[:, u % 2, :], bank[u][:, :], ACT.Gelu_apprx_tanh).then_inc(tile_evac, 1)
                act.wait_ge(tile_evac, j + (G0["U"] + 1))
                act.dma_start(act_dram[j, :, :], actb[:, u % 2, :]).then_inc(act_out[u % 2], 16)

            def u_iteration(i):
                for u in range(4):
                    ahead(G0["U"], u, i)
                    act_tile(i * 4 + u, u, i * 32 + 16 * (u // 2))

            for tb in range(TB):
                if tb == 0:
                    for u in range(4):
                        ahead(G0["U"], u)
                        act_tile(u, u, 16 * (u // 2) if u >= 2 else None)
                    u_iteration(1)
                else:
                    with act.Fori(0, U_LEAD - 1) as i:
                        u_iteration(i + U_LEAD * tb)
                act.wait_ge(tk_diff, tb + 1)
                nc.scalar.activation(bv[:, :, :], bv[:, :, :], ACT.Exp).then_inc(tk_exp, 1)
                u_iteration(U_LEAD * tb + U_LEAD - 1)

            def g_group(q, buf, t0, first=None):
                act.wait_ge(g_done, q + 1)
                if first is not None:
                    act.wait_ge(g_out[buf], first)
                b = (t0 // 4) % 4
                nc.scalar.activation(GS[:, buf, :, t0:t0 + 4],
                                     bank[4 + b][:, :].rearrange("p (t j) -> p j t", t=4), ACT.Copy)\
                    .then_inc(g_evac, 1)

            def gate_block(i, pairs):
                for half in range(2):
                    for k in range(2):
                        for u in range(4):
                            it = i * 4 + (TB * U_LEAD + 2 * half + k)
                            ahead(G0["U"], u, it)
                            act_tile(it * 4 + u, u, it * 32 + 16 * (u // 2))
                            for e in range(2):
                                n = 8 * k + 2 * u + e
                                first = None
                                if n == 0 and pairs:
                                    first = i * 16
                                g_group(i * 32 + (16 * half + n), half, 4 * n, first)

            gate_block(0, False)
            with act.Fori(1, 4) as i:
                gate_block(i, True)
            with act.Fori(TB * U_LEAD + U_GATE, 32) as i:
                u_iteration(i)

            def pw_tile(j, slot):
                act.wait_ge(pw, j + 1)
                nc.scalar.activation(WH[:, slot, :], AJ[:, slot, :], ACT.Copy).then_inc(pw_hi, 1)

            for u in range(4):
                pw_tile(u, u)
                ahead(G0["V"], u)
            with act.Fori(1, 32) as i:
                for u in range(4):
                    pw_tile(i * 4 + u, u)
                    ahead(G0["V"], u, i)

            norm_squares(X, S, block_ready=(res_done, 0))
            norm_root(S, 0)
            for kb in range(KB):
                done_blocks[0] += 1
                act.wait_ge(n_scaled, done_blocks[0])
                nc.scalar.activation(X[:, kb, :], T[:, kb, :], ACT.Identity, scale=col("fin1", kb)).then_inc(n_aff, 1)
            for kb in range(KB):
                act.wait_ge(n_aff, done_blocks[0] - KB + kb + 1)
                nc.scalar.activation(T[:, kb, :], X[:, kb, :], ACT.Square).then_inc(n_sq, 1)
            norm_root(S)
            norm_apply(S, lambda kb: col("mix2", kb), None, HH)
            for g in range(G0["aq"], G0["rg"]):
                ahead(g, 0)

            def at2_evac(n, it):
                act.wait_ge(at_t, it * 16 + (32 + n + 1))
                if n >= 2:
                    act.wait_ge(at_av, it * 16 + (32 + n - 1))
                b = n % 2
                nc.scalar.activation(APT[:, b, :, :].rearrange("p k q -> p (k q)"), bank[2 * b][:, 0:256], ACT.Copy)\
                    .then_inc(at_pt, 1)

            def at2_hi(n, it):
                act.wait_ge(at_av, it * 16 + (32 + n + 1))
                m, r, a = n // 8, n // 4 % 2, n % 4
                rr = slice(64 * r, 64 * r + 64)
                nc.scalar.activation(ATH[rr, bass.ds(it * 2 + m, 1), a * P:(a + 1) * P]
                                     .rearrange("p o q -> p (o q)"),
                                     bank[2 * (n % 2) + 1][rr, 256:384], ACT.Copy).then_inc(at_hi, 1)

            def at2_sink(n, it):
                act.wait_ge(at_masked, it * 16 + (32 + n + 1))
                m, r = n // 8, n // 4 % 2
                nc.scalar.activation(amx[:, n % 3, 3:4], amx[:, n % 3, 2:3], ACT.Exp).then_inc(at_exp, 1)

            with act.Fori(0, 2) as it:
                for n in range(16 + 3):
                    if n < 16:
                        at2_sink(n, it)
                        nc.scalar.activation(AS[:, n % 3, :], AS[:, n % 3, :], ACT.Exp, bias=amx[:, n % 3, 0:1],
                                             accum_out=amx[:, n % 3, 1:2]).then_inc(at_exp, 1)
                    if 2 <= n < 18:
                        at2_evac(n - 2, it)
                    if n >= 3:
                        at2_hi(n - 3, it)
            for k in range(8):
                act.wait_ge(gn_cen, k + 1)
                if k == 0:
                    act.wait_ge(at_lo, 64)
                    act.wait_ge(r_pv, 16)
                nc.scalar.activation(T[:, k, :], OT[:, k, :], ACT.Square).then_inc(gn_sq, 1)
            for h in range(4):
                act.wait_ge(gn_var, h + 1)
                nc.scalar.activation(rst4[:, h, :], bank[4 + h][:, :], ACT.Sqrt, bias=eps[:, 0:1], scale=1.0 / 256)\
                    .then_inc(gn_root, 1)
            for k in range(8):
                ahead(G0["rg"], k)
                tile_ready(G0["rg"] + k)
                nc.scalar.activation(T[:, k, :], bank[(G0["rg"] + k) % R][:, :], ACT.Silu).then_inc(tile_evac, 1)
                act.wait_ge(rg_mul, k + 1)
                nc.scalar.activation(RH[:, k, :], T[:, k, :], ACT.Copy).then_inc(rg_hi, 1)
            for k in range(8):
                ahead(G0["ga2"], k)
                tile_ready(G0["ga2"] + k)
                act.wait_ge(rg_lo, k + 1)
                nc.scalar.activation(T[:, k, :], bank[(G0["ga2"] + k) % R][:, :], ACT.Sigmoid).then_inc(tile_evac, 1)
            for k in range(4):
                ahead(G0["atto"], k)
            for k in range(8):
                ahead(G0["gr2"], k)
                tile_ready(G0["gr2"] + k)
                if k == 0:
                    act.wait_ge(tile_evac, evac_before(G0["gr2"]))
                nc.scalar.activation(OT[:, k, :], bank[(G0["gr2"] + k) % R][:, :], ACT.Sigmoid).then_inc(tile_evac, 1)
            for k in range(8):
                ahead(G0["reto"], k)
                act.wait_ge(mg_m, KB + k + 1)
                if k == 0:
                    act.wait_ge(tile_done, G0["reto"])
                nc.scalar.activation(HH[:, k, :], T[:, k, :], ACT.Copy).then_inc(mg_hi, 1)
            for k in range(8):
                ahead(G0["out2"], k)
            norm_squares(X, S, ready=[(mg_lo, 2 * KB)],
                         block_ready=(tile_evac, evac_before(G0["out2"])))
            norm_root(S)
            norm_apply(S, lambda kb: col("ffn2", kb), None, HH)
            def ffn_body(i, peeled):
                for u in range(4):
                    g = i * 4 + (G0["gateup"] + u)
                    ahead(G0["gateup"], u, i)
                    if u % 2 == 0:
                        tile_ready(g)
                        if not peeled:
                            act.wait_ge(ff_lo, i * 2 + (u // 2 - 1))
                        nc.scalar.activation(T[:, u // 2, :], bank[(G0["gateup"] + u) % R][:, :], ACT.Silu)\
                            .then_inc(tile_evac, 1)
                    else:
                        act.wait_ge(ff_mul, i * 2 + (u // 2 + 1))
                        nc.scalar.activation(FH[:, bass.ds(i * 2 + u // 2, 1), :].rearrange("p o t -> p (o t)"),
                                             T[:, u // 2, :], ACT.Copy).then_inc(tile_evac, 1)

            ffn_body(0, True)
            with act.Fori(1, FB // 2) as i:
                ffn_body(i, False)
            for k in range(FB):
                ahead(G0["down"], k)
            norm_squares(X, S, block_ready=(res_done, KB))
            norm_root(S, 0)
            for kb in range(KB):
                done_blocks[0] += 1
                act.wait_ge(n_scaled, done_blocks[0])
                nc.scalar.activation(T[:, kb, :], T[:, kb, :], ACT.Identity, scale=col("fin2", kb))\
                    .then_inc(out_rdy, 1)

        @block.tensor
        def _(pe):
            def three(out_, ah, al, bh, bl, first, last, **kw):
                pe.matmul(out_, ah, bh, start=first, stop=False, **kw)
                pe.matmul(out_, ah, bl, start=False, stop=False, **kw)
                return pe.matmul(out_, al, bh, start=False, stop=last, **kw)

            def tile_wait(g, e):
                pe.wait_ge(w_lo, g + 1)
                pe.wait_ge(tile_evac, e - R + 1)

            def columns(g, slot, e, xh=HH, xl=HL, first=False, split=None):
                if first:
                    pe.wait_ge(w_lo, g + 1)
                else:
                    tile_wait(g, e)
                for kb in range(KB):
                    if split:
                        pe.wait_ge(split[0], split[1] + kb + 1)
                    mm = three(bank[slot][:, :], whi[:, slot, kb, :], wlo[:, slot, kb, :], xh[:, kb, :], xl[:, kb, :],
                               kb == 0, kb == KB - 1)
                return mm

            def rows(b0, slot, part, xh, xl, blocks):
                wh = whi[:, slot, :, :].rearrange("p k c -> p (k c)")
                wl = wlo[:, slot, :, :].rearrange("p k c -> p (k c)")
                for b in range(blocks):
                    for k in range(2):
                        x = (slice(0, P), 2 * part + k, slice(b * P, (b + 1) * P))
                        w = (slice(0, P), slice(k * S, (k + 1) * S))
                        mm = three(bank[b0 + b][:, :], xh[x], xl[x], wh[w], wl[w], part == 0 and k == 0,
                                   part == 3 and k == 1)
                return mm

            def rows_one(out_, slot, xh, xl, blocks):
                for b in range(blocks):
                    for kb in range(KB):
                        mm = three(out_[:, b * P:(b + 1) * P], xh[:, kb, b * P:(b + 1) * P],
                                   xl[:, kb, b * P:(b + 1) * P], whi[:, slot, kb, :], wlo[:, slot, kb, :],
                                   kb == 0, kb == KB - 1)
                return mm

            blocks = [0]

            def norm_sum(width, b=4):
                for kb in range(KB):
                    blocks[0] += 1
                    pe.wait_ge(n_sq, blocks[0])
                    mm = pe.matmul(bank[b][:, 0:width], ones[:, :], T[:, kb, 0:width], start=(kb == 0),
                                   stop=(kb == KB - 1))
                mm.then_inc(n_sum, 1)

            def ada_tile(a, slot, turns, k):
                pe.wait_ge(ada_in[slot], turns)
                for kb in range(KB):
                    mm = pe.matmul(bank[7][:, 2 * k:2 * k + 2], adaw[:, slot, kb, :], scc[:, kb, :], start=(kb == 0),
                                   stop=(kb == KB - 1))
                mm.then_inc(ada_used, 1)

            pe.wait_ge(const_in, CONST0)
            norm_sum(S)
            pe.wait_ge(silu_c, 1)
            for unit in range(2):
                if unit:
                    pe.wait_ge(ada_evac, unit)
                for k in range(8):
                    ada_tile(8 * unit + k, k % R, 16 * (2 * unit + k // R + 1), k)
            for u in range(4):
                if u == 3:
                    norm_sum(CTX)
                columns(G0["q"] + u, u, 0, first=True, split=(n_lo, 0) if u == 0 else None).then_inc(tile_done, 1)
            pe.wait_ge(n_lo, 2 * KB)
            for u in range(4):
                columns(G0["k"] + u, u, G0["k"] + u)
                for kb in range(KB):
                    mm = three(bank[4 + u][:, 0:CTX], whi[:, u, kb, :], wlo[:, u, kb, :], CH[:, kb, :], CL[:, kb, :],
                               kb == 0, kb == KB - 1)
                mm.then_inc(tile_done, 1)
            pe.wait_ge(tile_evac, G0["v"])
            for u in range(4):
                pe.wait_ge(w_lo, G0["v"] + u + 1)
                rows(0, u, u, HH, HL, TB)
                rows(4, u, u, CH, CL, 2).then_inc(tile_done, 1)

            pe.wait_ge(const2_in, 32)
            pe.wait_ge(tile_evac, G0["gu"])

            def at1_scores(n, it):
                pair, hh, a = n // 8, n // 4 % 2, n % 4
                b = n % 2
                if n >= 2:
                    pe.wait_ge(at_masked, it * 16 + (n - 1))
                r = slice(64 * hh, 64 * hh + 64)
                q = QT[r, 2 * it + pair, a * P:(a + 1) * P]
                k = KT[r, 2 * it + pair, :]
                pe.matmul(bank[4 + 2 * b][:, :], q, k[:, 0:S], start=True, stop=True)
                pe.matmul(bank[5 + 2 * b][:, 0:CTX], q, k[:, S:S + CTX], start=True, stop=True).then_inc(at_s, 1)

            def at1_turn(n, it):
                b = n % 2
                pe.wait_ge(at_p, it * 16 + (n + 1))
                if n >= 2:
                    pe.wait_ge(at_pt, it * 32 + 2 * (n - 1))
                    pe.wait_ge(at_lo, it * 16 + (n - 1))
                for k in range(6):
                    o = bank[2 * b + k // 4][:, (k % 4) * P:(k % 4 + 1) * P]
                    mm = pe.transpose(o, SS[:, n % 3, k * P:(k + 1) * P], ident[:, :])
                mm.then_inc(at_t, 1)

            def at1_values(n, it):
                pair, hh = n // 8, n // 4 % 2
                b = n % 2
                pe.wait_ge(at_pt, it * 32 + 2 * (n + 1))
                for k in range(6):
                    mm = pe.matmul(bank[2 * b + 1][64 * hh:64 * hh + 64, 256:384],
                                   VV[:, k, (4 * it + 2 * pair + hh) * HD:(4 * it + 2 * pair + hh + 1) * HD], PT[:, b, k, :], start=(k == 0), stop=(k == 5))
                mm.then_inc(at_av, 1)

            for it in range(2):
                for n in range(16 + 3):
                    if n < 16:
                        at1_scores(n, it)
                    if 2 <= n < 18:
                        at1_turn(n - 2, it)
                    if n >= 3:
                        at1_values(n - 3, it)

            pe.wait_ge(at_lo, 32)
            for u in range(4):
                columns(G0["gu"] + u, u, G0["gu"] + u).then_inc(tile_done, 1)
            for u in range(4):
                pe.wait_ge(w_lo, G0["gv"] + u + 1)
                rows(4, u, u, HH, HL, TB).then_inc(tile_done, 1)
            with pe.Fori(0, 4) as i:
                for u in range(4):
                    g = i * 4 + (G0["gates"] + u)
                    columns(g, u, g).then_inc(tile_done, 1)
                    if u == 0:
                        pe.wait_ge(ada_evac, i + 2)
                    for k in (2 * u, 2 * u + 1):
                        ada_tile(0, k % R, i * 32 + 16 * (4 + k // R + 1), k)
            pe.wait_ge(gm_vn, 4)
            pe.wait_ge(late_in, 48)
            pe.wait_ge(ada_evac, 6)
            for g in range(NH):
                for tb in range(TB):
                    mm = pe.matmul(bank[4 + g // 2][64 * (g % 2):64 * (g % 2) + 64, tb * P:(tb + 1) * P],
                                   GV[:, tb, 64 * g:64 * g + 64], wsT[:, g, :], start=True, stop=True)
            mm.then_inc(gm_mix, 1)

            def narrow(g, slot, e, xh, xl):
                tile_wait(g, e)
                for half in range(2):
                    for kb in range(4):
                        k = 4 * half + kb
                        mm = three(bank[slot + 4 * half][:, :], whi[:, slot, k, :], wlo[:, slot, k, :], xh[:, kb, :],
                                   xl[:, kb, :], kb == 0, kb == 3)
                mm.then_inc(tile_done, 1)

            pe.wait_ge(at_lo, 32)
            pe.wait_ge(gm_y, 4)
            for u in range(4):
                narrow(G0["pa"] + u, u, G0["pa"] + u, YAH, YAL)
            pe.wait_ge(gm_lo, 4)
            for u in range(4):
                narrow(G0["pb"] + u, u, G0["pb"] + u, YBH, YBL)
            def layer(name, split, e0=0, xh=HH, xl=HL):
                for u in range(4):
                    g = G0[name] + u
                    columns(g, g % R, g - e0, xh, xl, split=split if u == 0 else None).then_inc(tile_done, 1)
                if COUNT[name] > 4:
                    with pe.Fori(1, COUNT[name] // 4) as i:
                        for u in range(4):
                            t = G0[name] + u
                            columns(i * 4 + t, t % R, i * 4 + (t - e0), xh, xl).then_inc(tile_done, 1)

            layer("out", (mg_lo, 0))
            norm_sum(S)
            layer("wq", (n_lo, 2 * KB))
            pe.wait_ge(tile_evac, G0["U"])
            pe.wait_ge(keys_in, 16)
            for n in range(16):
                tb, quad = n // 4, n % 4
                if n >= 4:
                    pe.wait_ge(sc_evac, n - 3)
                for k in range(4):
                    hp = 4 * quad + k
                    mm = pe.matmul(bank[4 + quad][:, k * P:(k + 1) * P], QP[:, hp, tb * P:(tb + 1) * P],
                                   keysT[:, hp, :], start=True, stop=True)
                mm.then_inc(sc_done, 1)

            def u_tile(g, slot):
                columns(g, slot, g).then_inc(tile_done, 1)

            for tb in range(TB):
                with pe.Fori(0, U_LEAD) as i:
                    for u in range(4):
                        u_tile(i * 4 + (G0["U"] + 4 * U_LEAD * tb + u), u)
                pe.wait_ge(tk_sel, tb + 1)
                if tb == 0:
                    pe.wait_ge(sc_evac, 16)
                else:
                    pe.wait_ge(tk_it, tb)
                for k in range(3):
                    mm = pe.transpose(bank[4][:, k * P:(k + 1) * P], sel3[:, k, :], ident[:, :])
                mm.then_inc(tk_tr, 1)
            pe.wait_ge(tk_it, TB)

            def gate_group(q, n, half, peeled=False):
                pe.wait_ge(oh_ready, q + 1)
                if not peeled:
                    pe.wait_ge(g_evac, q - 3)
                b = bank[4 + n % 4]
                for e in range(4):
                    s = 4 * half + e
                    pe.matmul(b[:, e * P:(e + 1) * P], A1[:, s, :], B1[:, s, :], start=True, stop=False)
                    mm = pe.matmul(b[:, e * P:(e + 1) * P], A2[:, s, :], B1[:, s, :], start=False, stop=True)
                mm.then_inc(g_done, 1)

            gu0 = G0["U"] + 4 * TB * U_LEAD
            for u in range(4):
                u_tile(gu0 + u, u)
                for k in range(2):
                    gate_group(2 * u + k, 2 * u + k, k, peeled=(2 * u + k < 4))
            with pe.Fori(1, U_GATE) as i:
                for u in range(4):
                    u_tile(i * 4 + (gu0 + u), u)
                    for k in range(2):
                        gate_group(i * 8 + (2 * u + k), 2 * u + k, k)
            with pe.Fori(0, U_TAIL) as i:
                for u in range(4):
                    u_tile(i * 4 + (gu0 + 4 * U_GATE + u), u)

            def add_up(slot, xh, xl, first, last):
                for kb in range(KB):
                    mm = three(bank[kb][:, :], whi[:, slot, kb, :], wlo[:, slot, kb, :], xh, xl, first, last)
                mm.then_inc(tile_done, 1)

            def v_tile(j, u, first=False, last=False):
                pe.wait_ge(w_lo, j + (G0["V"] + 1))
                pe.wait_ge(pw_lo, j + 1)
                add_up(u, WH[:, u, :], WL[:, u, :], first, last)

            pe.wait_ge(tile_evac, G0["V"])
            pe.wait_ge(g_evac, P)
            for u in range(4):
                v_tile(u, u, first=(u == 0))
            with pe.Fori(1, 31) as i:
                for u in range(4):
                    v_tile(i * 4 + u, u)
            for u in range(4):
                v_tile(124 + u, u, last=(u == 3))

            norm_sum(S, 0)
            norm_sum(S)
            e0 = COUNT["V"]
            layer("aq", (n_lo, 3 * KB), e0)
            with pe.Fori(1, 3) as i:
                for u in range(4):
                    g = i * 4 + (G0["aq"] + u)
                    columns(g, u, g - e0).then_inc(tile_done, 1)
            for h in range(2):
                if h:
                    pe.wait_ge(tile_evac, evac_before(G0["rv"]))
                for u in range(4):
                    pe.wait_ge(w_lo, G0["rv"] + 4 * h + u + 1)
                    rows(4 - 4 * h, u, u, HH, HL, TB).then_inc(tile_done, 1)
            tile_wait(G0["av"], G0["rv"] + 4 - e0 + 3)
            rows_one(bank[4], 0, HH, HL, TB).then_inc(tile_done, 1)
            columns(G0["ak"], 1, G0["ak"] - e0).then_inc(tile_done, 1)

            pe.wait_ge(tile_evac, evac_before(G0["rg"]))

            def at2_scores(n, it):
                m, r, a = n // 8, n // 4 % 2, n % 4
                b = n % 2
                if n >= 2:
                    pe.wait_ge(at_masked, it * 16 + (32 + n - 1))
                rr = slice(64 * r, 64 * r + 64)
                k0, k1 = (a - 1) * P if a else 0, (a + 1) * P
                pe.matmul(bank[4 + b][:, 256 - (k1 - k0):256], AQ[rr, 2 * it + m, a * P:(a + 1) * P], AK[rr, k0:k1],
                          start=True, stop=True).then_inc(at_s, 1)

            def at2_turn(n, it):
                b = n % 2
                pe.wait_ge(at_p, it * 16 + (32 + n + 1))
                if n >= 2:
                    pe.wait_ge(at_pt, it * 16 + (64 + n - 1))
                for k in range(2):
                    mm = pe.transpose(bank[2 * b][:, k * P:(k + 1) * P], AS[:, n % 3, k * P:(k + 1) * P], ident[:, :])
                mm.then_inc(at_t, 1)

            def at2_values(n, it):
                r, a = n // 4 % 2, n % 4
                b = n % 2
                pe.wait_ge(at_pt, it * 16 + (64 + n + 1))
                if n >= 2:
                    pe.wait_ge(at_lo, it * 16 + (32 + n - 1))
                for k in range(2):
                    kb = max(a - 1 + k, 0)
                    mm = pe.matmul(bank[2 * b + 1][64 * r:64 * r + 64, 256:384], AV[:, kb, 64 * r:64 * r + 64],
                                   APT[:, b, k, :], start=(k == 0), stop=(k == 1))
                mm.then_inc(at_av, 1)

            for it in range(2):
                for n in range(16 + 3):
                    if n < 16:
                        at2_scores(n, it)
                    if 2 <= n < 18:
                        at2_turn(n - 2, it)
                    if n >= 3:
                        at2_values(n - 3, it)
            pe.wait_ge(at_lo, 64)
            for h in range(4):
                for J in range(TB + 1):
                    if J < TB:
                        n = 4 * h + J
                        if n >= 2:
                            pe.wait_ge(r_sd, n - 1)
                        pe.matmul(bank[4 + J % 2][:, 0:S - J * P], RK[:, h, J * P:(J + 1) * P], RQ[:, h, J * P:S],
                                  start=True, stop=True).then_inc(r_s, 1)
                    if J:
                        K = J - 1
                        pe.wait_ge(r_sd, 4 * h + K + 1)
                        if K == 0 and h >= 2:
                            pe.wait_ge(r_oc, h - 1)
                        for vb in range(2):
                            mm = pe.matmul(bank[2 * (h % 2) + vb][:, K * P:S],
                                           RV[:, K, h * 256 + vb * P:h * 256 + (vb + 1) * P],
                                           RSC[:, K % 2, 0:S - K * P], start=(K == 0), stop=(K == TB - 1),
                                           skip_group_check=True)
                        mm.then_inc(r_pv, 1)
            for h in range(4):
                pe.wait_ge(r_oc, h + 1)
                for vb in range(2):
                    mm = pe.matmul(bank[4 + h][:, :], ones[:, :], OT[:, 2 * h + vb, :], start=(vb == 0), stop=(vb == 1))
                mm.then_inc(gn_mu, 1)
            for h in range(4):
                pe.wait_ge(gn_sq, 2 * h + 2)
                for vb in range(2):
                    mm = pe.matmul(bank[4 + h][:, :], ones[:, :], T[:, 2 * h + vb, :], start=(vb == 0), stop=(vb == 1))
                mm.then_inc(gn_var, 1)

            def columns2(name, n):
                with pe.Fori(0, n // 4) as i:
                    for u in range(4):
                        t = G0[name] + u
                        columns(i * 4 + t, t % R, i * 4 + (t - e0)).then_inc(tile_done, 1)

            pe.wait_ge(r_oc, 4)
            columns2("rg", 8)
            columns2("ga2", 8)
            pe.wait_ge(gn_root, 4)
            for u in range(4):
                g = G0["atto"] + u
                narrow(g, g % R, g - e0, ATH, ATL)
            columns2("gr2", 8)
            pe.wait_ge(rg_lo, 8)
            layer("reto", None, e0, RH, RL)
            layer("out2", (mg_lo, KB), e0)
            norm_sum(S)
            layer("gateup", (n_lo, 4 * KB), e0)
            pe.wait_ge(tile_evac, evac_before(G0["down"]))

            def down(f, t, first=False, last=False):
                pe.wait_ge(w_lo, f + (G0["down"] + 1))
                pe.wait_ge(ff_lo, f + 1)
                xh = FH[:, bass.ds(f, 1), :].rearrange("p o t -> p (o t)")
                xl = FL[:, bass.ds(f, 1), :].rearrange("p o t -> p (o t)")
                add_up(t % R, xh, xl, first, last)

            down(0, G0["down"], first=True)
            with pe.Fori(0, (FB - 2) // 4) as i:
                for u in range(4):
                    down(i * 4 + (1 + u), G0["down"] + 1 + u)
            down(FB - 1, G0["down"] + FB - 1, last=True)
            norm_sum(S, 0)

        @block.vector
        def _(v):
            chain = Tally()

            def then(ins):
                ins.then_inc(dve, 1)
                chain.add()
                v.wait_ge(dve, chain.at())

            scaled = [0, 0, 0]

            def norm_rstd(width):
                scaled[0] += 1
                v.wait_ge(n_root, scaled[0])
                then(nc.vector.reciprocal(rstd[:, 0:width], rms[:, 0:width]))

            def norm_scale(src, width):
                for kb in range(KB):
                    nc.vector.tensor_tensor(T[:, kb, 0:width], src[:, kb, :], rstd[:, 0:width], ALU.mult)\
                        .then_inc(n_scaled, 1)

            def norm_low(width, H, L):
                for kb in range(KB):
                    scaled[2] += 1
                    v.wait_ge(n_hi, scaled[2])
                    nc.vector.tensor_tensor(L[:, kb, :], T[:, kb, 0:width], H[:, kb, :].bitcast(F32), ALU.subtract)\
                        .then_inc(n_lo, 1)

            def ada_rows(unit):
                v.wait_ge(ada_used, unit * 8 + 8)
                a = COLS["adab"][0]
                nc.vector.tensor_tensor(mod[:, bass.ds(unit * 8, 8), :],
                                        bank[7][:, 0:16].rearrange("p (n c) -> p n c", c=2),
                                        bc(cols[:, bass.ds(unit * 8 + a, 8)], 2, 2), ALU.add).then_inc(ada_evac, 1)

            def gain_scale(k, chunk, who, name):
                a, b = COLS[name]
                nc.vector.scalar_tensor_tensor(gsc[:, k, :], mod[:, chunk:chunk + 8, who], 1.0, cols[:, a:b], ALU.add,
                                               ALU.mult).then_inc(gsc_ready, 1)

            nc.vector.memset(eps[:, :], EPS).then_inc(n_eps, 1)
            v.wait_ge(const_in, CONST0)
            for unit in range(2):
                ada_rows(unit)
            v.wait_ge(ada_evac, 2)
            gain_scale(0, 8, 0, "n1")
            gain_scale(1, 8, 1, "n1")
            norm_rstd(S)
            norm_scale(X, S)
            norm_low(S, HH, HL)

            def copy_tile(g, dst, src):
                v.wait_ge(tile_done, g + 1)
                return nc.vector.tensor_copy(dst, src)

            for u in range(3):
                copy_tile(u, QT[:, u, :], bank[u][:, :]).then_inc(tile_evac, 1)
            norm_rstd(CTX)
            norm_scale(CX, CTX)
            norm_low(CTX, CH, CL)
            copy_tile(3, QT[:, 3, :], bank[3][:, :]).then_inc(tile_evac, 1)
            for u in range(4):
                copy_tile(G0["k"] + u, KT[:, u, 0:S], bank[u][:, :])
                nc.vector.tensor_copy(KT[:, u, S:S + CTX], bank[4 + u][:, 0:CTX]).then_inc(tile_evac, 1)
            v.wait_ge(tile_done, G0["gu"])
            for b in range(6):
                ins = nc.vector.tensor_copy(VV[:, b, :], bank[b][:, :])
                if b >= 2:
                    ins.then_inc(tile_evac, 1)

            v.wait_ge(late_in, 16)

            def at1_mask(n, it):
                pair, hh, a = n // 8, n // 4 % 2, n % 4
                b = n % 2
                if n % 8 == 0:
                    v.wait_ge(bias_in[pair], it * 64 + 64)
                    for k in range(2):
                        e3 = E[:, pair, k, :].rearrange("p (m k) -> p m k", k=HD)
                        ins = nc.vector.tensor_tensor(e3, e3, bc(wmask[:, :], 1, 14), ALU.add)
                    then(ins)
                v.wait_ge(at_s, it * 16 + (n + 1))
                if n >= 3:
                    v.wait_ge(at_t, it * 16 + (n - 2))
                m0, c = (6 - 2 * a) * HD, n % 3
                nc.vector.scalar_tensor_tensor(SS[:, c, 0:S], bank[4 + 2 * b][:, :], SCALE, E[:, pair, hh, m0:m0 + S],
                                               ALU.mult, ALU.add)
                then(nc.vector.tensor_scalar(SS[:, c, S:S + CTX], bank[5 + 2 * b][:, 0:CTX], SCALE, None, ALU.mult))
                nc.vector.tensor_reduce(mx[:, c, 0:1], SS[:, c, :], AX_X, ALU.max, negate=True).then_inc(at_masked, 1)

            def at1_prob(n, it):
                c = n % 3
                v.wait_ge(at_exp, it * 16 + (n + 1))
                then(nc.vector.reciprocal(mx[:, c, 2:3], mx[:, c, 1:2]))
                nc.vector.tensor_scalar(SS[:, c, :], SS[:, c, :], mx[:, c, 2:3], None, ALU.mult).then_inc(at_p, 1)

            def at1_low(n, it):
                pair, hh, a = n // 8, n // 4 % 2, n % 4
                v.wait_ge(at_hi, it * 16 + (n + 1))
                r = slice(64 * hh, 64 * hh + 64)
                dst = YAL[r, bass.ds(it * 2 + pair, 1), a * P:(a + 1) * P].rearrange("p o q -> p (o q)")
                h = YAH[r, bass.ds(it * 2 + pair, 1), a * P:(a + 1) * P].rearrange("p o q -> p (o q)").bitcast(F32)
                nc.vector.tensor_tensor(dst, bank[2 * (n % 2) + 1][r, 256:384], h, ALU.subtract).then_inc(at_lo, 1)

            chain_loop(v, chain, 2, 2 + 16 * 2, lambda it: [
                (at1_mask(n, it) if n < 16 else None, at1_prob(n - 1, it) if 1 <= n <= 16 else None,
                 at1_low(n - 3, it) if n >= 3 else None) for n in range(16 + 3)])

            v.wait_ge(tile_evac, G0["gates"])
            for tb in range(TB):
                ins = nc.vector.bn_stats(bn[:, tb, :], GV[:, tb, :])
            then(ins)
            for tb in range(TB):
                ins = nc.vector.bn_aggr(st[:, 2 * tb + 16:2 * tb + 18], bn[:, tb, :])
            then(ins)
            for tb in range(TB):
                nc.vector.tensor_copy(st[:, 4 + tb:5 + tb], st[:, 2 * tb + 17:2 * tb + 18]).then_inc(gm_var, 1)
            v.wait_ge(gm_root, 1)
            then(nc.vector.reciprocal(st[:, 12:16], st[:, 8:12]))
            for tb in range(TB):
                nc.vector.tensor_scalar(GV[:, tb, :], GV[:, tb, :], st[:, 2 * tb + 16:2 * tb + 17],
                                        st[:, 12 + tb:13 + tb], ALU.subtract, ALU.mult).then_inc(gm_vn, 1)
            with v.Fori(2, 6) as i:
                ada_rows(i)
            v.wait_ge(ada_evac, 6)
            gain_scale(2, 32, 0, "n2")
            v.wait_ge(gm_mix, 1)
            v.wait_ge(late_in, 48)
            for b in range(4):
                then(nc.vector.scalar_tensor_tensor(
                    MX[:, b, :].rearrange("p (c q) -> p c q", c=TB), bank[4 + b][:, :].rearrange("p (c q) -> p c q", c=TB),
                    col("lng", b), bc(bsb[:, b, :], 1, TB), ALU.mult, ALU.add))
                nc.vector.tensor_tensor(MX[:, b, :], MX[:, b, :], UT[:, b, :], ALU.mult).then_inc(gm_y, 1)
            for b in range(4):
                v.wait_ge(gm_hi, b + 1)
                nc.vector.tensor_tensor(YBL[:, b, :], MX[:, b, :], YBH[:, b, :].bitcast(F32), ALU.subtract)\
                    .then_inc(gm_lo, 1)
            v.wait_ge(tile_evac, G0["pa"])
            v.wait_ge(gm_lo, 4)
            for u in range(4):
                v.wait_ge(tile_done, G0["pa"] + u + 1)
                nc.vector.tensor_tensor(T[:, 2 * u, :], bank[u][:, :], SG[:, 2 * u, :], ALU.mult)
                nc.vector.tensor_tensor(T[:, 2 * u + 1, :], bank[4 + u][:, :], SG[:, 2 * u + 1, :], ALU.mult)\
                    .then_inc(tile_evac, 1)

            def split_merged(k, h0):
                v.wait_ge(mg_hi, h0 + k + 1)
                nc.vector.tensor_tensor(HL[:, k, :], T[:, k, :], HH[:, k, :].bitcast(F32), ALU.subtract)\
                    .then_inc(mg_lo, 1)

            for u in range(4):
                v.wait_ge(tile_done, G0["pb"] + u + 1)
                nc.vector.tensor_tensor(SG[:, 8 + 2 * u, :], bank[u][:, :], SG[:, 8 + 2 * u, :], ALU.mult)
                ins = nc.vector.tensor_tensor(SG[:, 9 + 2 * u, :], bank[4 + u][:, :], SG[:, 9 + 2 * u, :], ALU.mult)
                ins.then_inc(tile_evac, 1)
                v.wait_ge(tile_evac, G0["pb"] + u + 1)
                for k in (2 * u, 2 * u + 1):
                    nc.vector.tensor_tensor(T[:, k, :], T[:, k, :], SG[:, 8 + k, :], ALU.add).then_inc(mg_m, 1)
                if u:
                    split_merged(2 * u - 2, 0)
                    split_merged(2 * u - 1, 0)
            split_merged(6, 0)
            split_merged(7, 0)

            def residual(ps, kb, gate):
                xk = X[:, kb, :]
                if gate is None:
                    return nc.vector.tensor_tensor(xk, ps, xk, ALU.add)
                return nc.vector.scalar_tensor_tensor(xk, ps, gate, xk, ALU.mult, ALU.add)

            for k in range(8):
                v.wait_ge(tile_done, G0["out"] + k + 1)
                residual(bank[k % R][:, :], k, mod[:, 16 + k, 0:1]).then_inc(tile_evac, 1)
            norm_rstd(S)
            norm_scale(X, S)
            norm_low(S, HH, HL)

            def topk(tb):
                v.wait_ge(sc_evac, tb * 4 + 4)
                then(nc.vector.tensor_copy(SSc, SC[:, tb, :, :]))

                def sixteen(lists, values, indices, count):
                    for n in range(count):
                        ins = nc.vector.max(values(n)[:, 0:8], lists(n))
                    then(ins)
                    for n in range(count):
                        ins = nc.vector.max_index(indices(n)[:, 0:8], values(n)[:, 0:8], lists(n))
                    then(ins)
                    for n in range(count):
                        ins = nc.vector.match_replace(lists(n), values(n)[:, 0:8], lists(n), MASKED)
                    then(ins)
                    for n in range(count):
                        ins = nc.vector.max(values(n)[:, 8:16], lists(n))
                    then(ins)
                    for n in range(count):
                        ins = nc.vector.max_index(indices(n)[:, 8:16], values(n)[:, 8:16], lists(n))
                    then(ins)

                sixteen(lambda n: SSc[:, n, :], lambda n: small[:, n, :], lambda n: tki[:, n, :], 16)
                nc.vector.tensor_copy(tkf[:, :, :], tki[:, :, :])
                halves = small[:, :, :].rearrange("p (h w) a -> p w h a", w=2)
                then(nc.vector.tensor_tensor(cand, bc(halves[:, 0], 3, 16), bc(halves[:, 1], 2, 16), ALU.add))
                c2 = cand.rearrange("p h a b -> p h (a b)")
                sixteen(lambda h: c2[:, h, :], lambda h: bv[:, h, :], lambda h: bp[:, h, :], NH)
                nc.vector.tensor_scalar(bab[:, 0, :, :], bp[:, :, :], 4, None, ALU.logical_shift_right)
                nc.vector.tensor_scalar(bab[:, 1, :, :], bp[:, :, :], 15, None, ALU.bitwise_and)
                then(nc.vector.tensor_copy(hs[:, 1, :], bv[:, :, 0]))
                nc.vector.tensor_tensor(bv[:, :, :], bv[:, :, :], bc(hs[:, 1, :], 2, 16), ALU.subtract)\
                    .then_inc(tk_diff, 1)
                then(nc.vector.tensor_copy(babf[:, :, :, :], bab[:, :, :, :]))
                idx = tkf[:, :, :].rearrange("p (h w) a -> p w h a", w=2)
                iota16 = bc(bc(iota[:, 0:16], 1, 16), 1, NH)
                for w in range(2):
                    then(nc.vector.tensor_tensor(cand, bc(babf[:, w, :, :], 3, 16), iota16, ALU.is_equal))
                    then(nc.vector.tensor_tensor(cand, cand, bc(idx[:, w], 2, 16), ALU.mult))
                    ins = nc.vector.tensor_reduce(sel3[:, w, :].rearrange("p (h k) -> p h k", h=NH), cand, AX_X,
                                                  ALU.add)
                    then(ins)
                v.wait_ge(tk_exp, tb + 1)
                then(nc.vector.tensor_reduce(hs[:, 0, :], bv[:, :, :], AX_X, ALU.add))
                then(nc.vector.reciprocal(hs[:, 1, :], hs[:, 0, :]))
                nc.vector.tensor_tensor(sel3[:, 2, :].rearrange("p (h k) -> p h k", h=NH), bv[:, :, :],
                                        bc(hs[:, 1, :], 2, 16), ALU.mult).then_inc(tk_sel, 1)
                v.wait_ge(tk_tr, tb + 1)
                nc.vector.tensor_copy(IT[:, :, tb * P:(tb + 1) * P], bank[4][:, 0:3 * P].rearrange("p (k t) -> p k t", k=3))\
                    .then_inc(tk_it, 1)

            v.wait_ge(const2_in, 32)
            v.wait_ge(keys_in, 16)
            v.wait_ge(sc_done, 16)
            for tb in range(TB):
                topk(tb)
            v.wait_ge(tk_it, TB)
            then(nc.vector.tensor_copy(GH[:, :], IT[:, 2, :]))
            nc.vector.tensor_tensor(IT[:, 2, :], IT[:, 2, :], GH[:, :].bitcast(F32), ALU.subtract).then_inc(tk_gate, 1)
            v.wait_ge(tk_gate, 1)

            def onehots(q, half, peeled=False):
                if not peeled:
                    v.wait_ge(g_done, q - 1)
                for e in range(4):
                    i_t = IT[:, 0, bass.ds(q * 4 + e, 1)]
                    nc.vector.tensor_scalar(A1[:, 4 * half + e, :], iota[:, :], i_t,
                                            GH[:, bass.ds(q * 4 + e, 1)].bitcast(F32), ALU.is_equal, ALU.mult)
                    nc.vector.tensor_scalar(A2[:, 4 * half + e, :], iota[:, :], i_t,
                                            IT[:, 2, bass.ds(q * 4 + e, 1)], ALU.is_equal, ALU.mult)
                nc.vector.tensor_tensor(B1[:, 4 * half:4 * half + 4, :], bc(iota[:, :], 1, 4),
                                        bc(IT[:, 1, bass.ds(q * 4, 4)], 2, P), ALU.is_equal).then_inc(oh_ready, 1)

            for half in range(2):
                onehots(half, half, peeled=True)
            with v.Fori(1, P // 2) as i:
                for half in range(2):
                    onehots(i * 2 + half, half)

            def pw_tile(j, slot, turns, peeled=False):
                v.wait_ge(ag_in[slot], turns)
                if not peeled:
                    v.wait_ge(tile_done, j + (G0["V"] - R + 1))
                nc.vector.tensor_tensor(AJ[:, slot, :], AJ[:, slot, :],
                                        GJ[:, slot, :, :].rearrange("p b t -> p (b t)"), ALU.mult).then_inc(pw, 1)
                v.wait_ge(pw_hi, j + 1)
                nc.vector.tensor_tensor(WL[:, slot, :], AJ[:, slot, :], WH[:, slot, :].bitcast(F32), ALU.subtract)\
                    .then_inc(pw_lo, 1)

            for u in range(4):
                pw_tile(u, u, 32, peeled=True)
            with v.Fori(1, 32) as i:
                for u in range(4):
                    pw_tile(i * 4 + u, u, i * 32 + 32)
            v.wait_ge(tile_done, G0["aq"])
            for kb in range(KB):
                residual(bank[kb][:, :], kb, mod[:, 40 + kb, 0:1]).then_inc(res_done, 1)

            v.wait_ge(res_done, KB)
            norm_rstd(S)
            norm_scale(X, S)
            norm_rstd(S)
            norm_scale(X, S)
            norm_low(S, HH, HL)
            for k in range(4):
                v.wait_ge(tile_done, G0["aq"] + k + 1)
                nc.vector.tensor_scalar(AQ[:, k, :], bank[k][:, :], SCALE, None, ALU.mult).then_inc(tile_evac, 1)
            for k in range(4):
                copy_tile(G0["rq"] + k, RQ[:, k, :], bank[k][:, :]).then_inc(tile_evac, 1)
            for k in range(4):
                v.wait_ge(tile_done, G0["rk"] + k + 1)
                nc.vector.tensor_scalar(RK[:, k, :], bank[k][:, :], P ** -0.5, None, ALU.mult).then_inc(tile_evac, 1)
            for h in range(2):
                for b in range(TB):
                    copy_tile(G0["rv"] + 4 * h + 3, RV[:, b, h * S:(h + 1) * S], bank[4 - 4 * h + b][:, :])\
                        .then_inc(tile_evac, 1)
            copy_tile(G0["av"], AV[:, :, :], bank[4][:, :].rearrange("p (b c) -> p b c", b=TB)).then_inc(tile_evac, 1)
            copy_tile(G0["ak"], AK[:, :], bank[1][:, :]).then_inc(tile_evac, 1)

            v.wait_ge(alibi_in, 16)

            def at2_mask(n, it):
                m, r, a = n // 8, n // 4 % 2, n % 4
                b, c = n % 2, n % 3
                v.wait_ge(at_s, it * 16 + (32 + n + 1))
                if n >= 3:
                    v.wait_ge(at_t, it * 16 + (32 + n - 2))
                k0 = 0 if a else P
                if not a:
                    nc.vector.memset(AS[:, c, 0:P], NEG)
                slope = cols[:, bass.ds(it * 4 + (COLS["slope"][0] + 2 * m + r), 1)]
                sink = cols[:, bass.ds(it * 4 + (COLS["sink"][0] + 2 * m + r), 1)]
                then(nc.vector.scalar_tensor_tensor(AS[:, c, k0:256], alibi[:, k0:256], slope, bank[4 + b][:, k0:256],
                                                    ALU.mult, ALU.add))
                then(nc.vector.tensor_reduce(amx[:, c, 5:6], AS[:, c, :], AX_X, ALU.max))
                then(nc.vector.tensor_scalar(amx[:, c, 0:1], amx[:, c, 5:6], sink, -1.0, ALU.max, ALU.mult))
                nc.vector.tensor_tensor(amx[:, c, 2:3], amx[:, c, 0:1], sink, ALU.add).then_inc(at_masked, 1)

            def at2_prob(n, it):
                c = n % 3
                v.wait_ge(at_exp, it * 32 + (32 + 2 * n + 2))
                then(nc.vector.tensor_tensor(amx[:, c, 5:6], amx[:, c, 1:2], amx[:, c, 3:4], ALU.add))
                then(nc.vector.reciprocal(amx[:, c, 6:7], amx[:, c, 5:6]))
                nc.vector.tensor_scalar(AS[:, c, :], AS[:, c, :], amx[:, c, 6:7], None, ALU.mult).then_inc(at_p, 1)

            def at2_low(n, it):
                m, r, a = n // 8, n // 4 % 2, n % 4
                v.wait_ge(at_hi, it * 16 + (32 + n + 1))
                rr = slice(64 * r, 64 * r + 64)
                dst = ATL[rr, bass.ds(it * 2 + m, 1), a * P:(a + 1) * P].rearrange("p o q -> p (o q)")
                h = ATH[rr, bass.ds(it * 2 + m, 1), a * P:(a + 1) * P].rearrange("p o q -> p (o q)").bitcast(F32)
                nc.vector.tensor_tensor(dst, bank[2 * (n % 2) + 1][rr, 256:384], h, ALU.subtract).then_inc(at_lo, 1)

            chain_loop(v, chain, 2, 16 * 5, lambda it: [
                (at2_mask(n, it) if n < 16 else None, at2_prob(n - 1, it) if 1 <= n <= 16 else None,
                 at2_low(n - 3, it) if n >= 3 else None) for n in range(16 + 3)])

            for h in range(4):
                v.wait_ge(dec_in, 16 * (h + 1))
                for J in range(TB):
                    n = 4 * h + J
                    v.wait_ge(r_s, n + 1)
                    if n >= 2:
                        v.wait_ge(r_pv, n - 1)
                    nc.vector.tensor_tensor(RSC[:, J % 2, 0:S - J * P], bank[4 + J % 2][:, 0:S - J * P],
                                            DEC[:, 0:S - J * P], ALU.mult).then_inc(r_sd, 1)
                v.wait_ge(r_pv, 4 * h + 4)
                nc.vector.tensor_copy(OT[:, 2 * h, :], bank[2 * (h % 2)][:, :])
                nc.vector.tensor_copy(OT[:, 2 * h + 1, :], bank[2 * (h % 2) + 1][:, :]).then_inc(r_oc, 1)
            for h in range(4):
                v.wait_ge(gn_mu, h + 1)
                for vb in range(2):
                    o = OT[:, 2 * h + vb, :]
                    nc.vector.scalar_tensor_tensor(o, bank[4 + h][:, :], -1.0 / 256, o, ALU.mult, ALU.add)\
                        .then_inc(gn_cen, 1)
            for h in range(4):
                v.wait_ge(gn_root, h + 1)
                then(nc.vector.reciprocal(rst4[:, h, :], rst4[:, h, :]))
                for vb in range(2):
                    k = 2 * h + vb
                    nc.vector.scalar_tensor_tensor(OT[:, k, :], OT[:, k, :], col("gn", k), rst4[:, h, :], ALU.mult,
                                                   ALU.mult).then_inc(gn_done, 1)
            for k in range(8):
                v.wait_ge(tile_evac, evac_before(G0["rg"]) + k + 1)
                if k == 0:
                    v.wait_ge(gn_done, 8)
                nc.vector.tensor_tensor(T[:, k, :], T[:, k, :], OT[:, k, :], ALU.mult).then_inc(rg_mul, 1)
                v.wait_ge(rg_hi, k + 1)
                nc.vector.tensor_tensor(RL[:, k, :], T[:, k, :], RH[:, k, :].bitcast(F32), ALU.subtract)\
                    .then_inc(rg_lo, 1)
            for u in range(4):
                g = G0["atto"] + u
                v.wait_ge(tile_done, g + 1)
                if u == 0:
                    v.wait_ge(tile_evac, evac_before(g))
                nc.vector.tensor_tensor(T[:, 2 * u, :], bank[g % R][:, :], T[:, 2 * u, :], ALU.mult)
                nc.vector.tensor_tensor(T[:, 2 * u + 1, :], bank[4 + g % R][:, :], T[:, 2 * u + 1, :], ALU.mult)\
                    .then_inc(tile_evac, 1)
            for k in range(8):
                g = G0["reto"] + k
                v.wait_ge(tile_done, g + 1)
                v.wait_ge(tile_evac, evac_before(g))
                nc.vector.tensor_tensor(OT[:, k, :], bank[g % R][:, :], OT[:, k, :], ALU.mult).then_inc(tile_evac, 1)
                v.wait_ge(tile_evac, evac_before(g) + 1)
                nc.vector.tensor_tensor(T[:, k, :], T[:, k, :], OT[:, k, :], ALU.add).then_inc(mg_m, 1)
                if k:
                    split_merged(k - 1, KB)
            split_merged(7, KB)
            for k in range(8):
                g = G0["out2"] + k
                v.wait_ge(tile_done, g + 1)
                residual(bank[g % R][:, :], k, None).then_inc(tile_evac, 1)
            norm_rstd(S)
            norm_scale(X, S)
            norm_low(S, HH, HL)
            with v.Fori(0, FB // 2) as i:
                for k in range(2):
                    t = G0["gateup"] + 2 * k
                    v.wait_ge(tile_done, i * 4 + (t + 2))
                    v.wait_ge(tile_evac, i * 4 + (evac_before(t) + 1))
                    nc.vector.tensor_tensor(T[:, k, :], bank[(t + 1) % R][:, :], T[:, k, :], ALU.mult)\
                        .then_inc(ff_mul, 1)
                    v.wait_ge(tile_evac, i * 4 + (evac_before(t) + 2))
                    nc.vector.tensor_tensor(FL[:, bass.ds(i * 2 + k, 1), :].rearrange("p o t -> p (o t)"), T[:, k, :],
                                            FH[:, bass.ds(i * 2 + k, 1), :].rearrange("p o t -> p (o t)").bitcast(F32),
                                            ALU.subtract).then_inc(ff_lo, 1)
            v.wait_ge(tile_done, NT)
            for kb in range(KB):
                residual(bank[kb][:, :], kb, None).then_inc(res_done, 1)
            v.wait_ge(res_done, 2 * KB)
            norm_rstd(S)
            norm_scale(X, S)


def pack_tiles(inp):
    import numpy as np

    def blocks(w):
        k, n = w.shape
        return w.reshape(k // P, P, n // P, P).transpose(2, 1, 0, 3)

    def full(w):
        return blocks(w).reshape(-1, P, D)

    def half(w):
        b = blocks(w)
        return b.reshape(b.shape[0] // 2, 2, P, 4, P).transpose(0, 2, 1, 3, 4).reshape(-1, P, D)

    w1 = inp["w_in"][0]
    a, g = NH * HD, 512
    cuts = dict(q=w1[:, 0:a], k=w1[:, a:2 * a], v=w1[:, 2 * a:3 * a], gu=w1[:, 3 * a:3 * a + g],
                gv=w1[:, 3 * a + g:3 * a + 2 * g], gates=w1[:, 3 * a + 2 * g:])
    w2 = inp["w_in_2"][0]
    names = [("aq", 512), ("ak", 128), ("av", 128), ("rq", 512), ("rk", 512), ("rv", 1024), ("rg", 1024),
             ("ga2", 1024), ("gr2", 1024)]
    at = 0
    for name, n in names:
        cuts[name] = w2[:, at:at + n]
        at += n
    cuts["aq"] = cuts["aq"].reshape(D, 2, 4, HD).transpose(0, 2, 1, 3).reshape(D, 512)
    atto = inp["w_att_o_2"][0].reshape(2, 4, HD, D).transpose(1, 0, 2, 3).reshape(512, D)
    def pairs(w):
        return w.reshape(4, 2, P, -1, S).transpose(3, 0, 2, 1, 4).reshape(-1, P, D)

    parts = {name: (pairs if name in ("v", "gv", "rv") else full)(w) for name, w in cuts.items()}
    parts["pa"], parts["pb"], parts["atto"] = half(inp["w_proj_a"][0]), half(inp["w_proj_b"][0]), half(atto)
    parts["out"], parts["out2"], parts["reto"] = (full(inp[n][0]) for n in ("w_out", "w_out_2", "w_ret_o_2"))
    parts["wq"] = full(inp["peer_wq"][0])
    parts["U"] = inp["peer_u"][0].reshape(P, P, KB, P).transpose(1, 3, 2, 0).reshape(P, P, D)
    parts["V"] = inp["peer_v"][0].reshape(P, P, D).transpose(1, 0, 2)
    gate, up = full(inp["w_gate_2"][0]), full(inp["w_up_2"][0])
    parts["gateup"] = np.stack([gate, up], 1).reshape(-1, P, D)
    parts["down"] = inp["w_down_2"][0].reshape(FB, P, D)
    for name, n in PARTS:
        assert parts[name].shape == (n, P, D), (name, parts[name].shape)
    return np.concatenate([parts[name] for name, _ in PARTS])


def feature_rows(x):
    return x.reshape(x.shape[0], -1, P).transpose(2, 1, 0)


def pack(inp):
    import numpy as np

    f = np.float32

    def col(v):
        return v.reshape(-1, P).T

    sinks = inp["att_sinks_2"][0].reshape(2, 4).T.reshape(-1)
    slopes = (2.0 ** (-8.0 * (np.arange(8) + 1.0) / 8)).astype(f).reshape(2, 4).T.reshape(-1)
    tables = dict(n1=col(inp["norm1_g"][0]), n2=col(inp["norm2_g"][0]), fin1=col(inp["final_g"]),
                  mix2=col(inp["norm_mix_2"][0]), ffn2=col(inp["norm_ffn_2"][0]), fin2=col(inp["final_norm_2"]),
                  adab=col(inp["ada_b"][0]), lng=col(inp["gm_ln_g"][0]), gn=col(inp["ret_gn_gain_2"][0]),
                  sink=np.broadcast_to(sinks, (P, 8)), slope=np.broadcast_to(slopes, (P, 8)))
    rpb = np.zeros((8, 15, 127), f)
    rpb[:, :, 48:79] = inp["na_rpb"][0]
    qc, kc = np.arange(HD)[:, None], np.arange(HD)[None, :]
    start = np.clip(qc - 8, 0, HD - 16)
    window = np.where((kc >= start) & (kc < start + 16), 0.0, NEG).astype(f)
    i, j = np.arange(P)[:, None], np.arange(2 * P)[None, :]
    dist = i + P - j
    alibi = np.where((dist >= 0) & (dist < P), -dist, NEG).astype(f)
    ahead = np.arange(S)[None, :] - np.arange(P)[:, None]
    dec = np.stack([np.where(ahead >= 0, (1.0 - 2.0 ** (-5 - h)) ** np.maximum(ahead, 0), 0.0) for h in range(4)])
    bs = np.repeat(inp["gm_bs"][0].reshape(4, 2, 1, P), HD, axis=2)
    return dict(
        w=pack_tiles(inp),
        ada=inp["ada_w"][0].reshape(KB, P, 48, P).transpose(2, 1, 0, 3).reshape(48, P, D),
        x=feature_rows(inp["x"][0]), ctx=feature_rows(inp["ctx"][0]),
        c=np.stack([inp["c"][0].reshape(KB, P), inp["c_ctx"].reshape(KB, P)], -1).transpose(1, 0, 2),
        cols=np.concatenate([tables[n] for n in COLS], 1), ones=np.ones((P, P), f), ident=np.eye(P, dtype=f),
        iota=np.broadcast_to(np.arange(P, dtype=f), (P, P)), wmask=np.concatenate([window, window]), alibi=alibi,
        dec=dec.astype(f), rpb=np.broadcast_to(rpb, (HD, 8, 15, 127)), wsT=inp["gm_ws"][0].transpose(2, 0, 1),
        bs=bs.reshape(4, P, P).transpose(1, 0, 2), keys=inp["peer_keys"][0].reshape(16, P, P).transpose(2, 0, 1))


def kernel(**inputs):
    import numpy as np
    import concourse.bacc as bacc
    from concourse.bass_utils import run_bass_kernel_spmd

    nc = bacc.Bacc("TRN2", target_bir_lowering=False, num_devices=1)
    arrays, aps = {}, {}
    for name, a in pack({k: np.asarray(v) for k, v in inputs.items()}).items():
        a = np.ascontiguousarray(a)
        arrays[f"in_{name}"] = a
        aps[name] = nc.dram_tensor(f"in_{name}", a.shape, mybir.dt.from_np(a.dtype), kind="ExternalInput").ap()
    out = nc.dram_tensor("out_0", (P, KB, S), F32, kind="ExternalOutput").ap()
    build(nc, aps, out)
    r = run_bass_kernel_spmd(nc, [arrays], core_ids=[0])
    return r.results[0]["out_0"].transpose(2, 1, 0).reshape(1, S, D)
```

```python
from contextlib import ExitStack

import concourse.bass as bass
from concourse import mybir

F32 = mybir.dt.float32
FR = mybir.dt.float32r
U32 = mybir.dt.uint32
ALU = mybir.AluOpType
ACT = mybir.ActivationFunctionType
AX_X = mybir.AxisListType.X

P = 128
D = 1024
KB = D // P
S = 512
TB = S // P
CTX = 256
R = 4
EPS = 1e-6
NEG = -1e30
HD = 64
NH = 8
SCALE = HD ** -0.5
DFF = 2816
FB = DFF // P
WIN = 14 * 64

PARTS = [("q", 4), ("k", 4), ("v", 4), ("gu", 4), ("gv", 4), ("gates", 16), ("pa", 4), ("pb", 4), ("out", 8),
         ("wq", 16), ("U", 128), ("V", 128), ("aq", 4), ("rq", 4), ("rk", 4), ("rv", 8), ("av", 1), ("ak", 1),
         ("rg", 8), ("ga2", 8), ("atto", 4), ("gr2", 8), ("reto", 8), ("out2", 8), ("gateup", 2 * FB), ("down", FB)]
G0 = {}
NT = 0
for _name, _n in PARTS:
    G0[_name] = NT
    NT += _n
COUNT = dict(PARTS)
K_FORM = {"V", "down"}

COLS = {}
_c = 0
for _name, _n in [("n1", 8), ("n2", 8), ("fin1", 8), ("mix2", 8), ("ffn2", 8), ("fin2", 8), ("adab", 48), ("lng", 4),
                  ("gn", 8), ("sink", 8), ("slope", 8)]:
    COLS[_name] = (_c, _c + _n)
    _c += _n
NCOL = _c

RET_AT = (1, 8)
U_LEAD = 3
U_GATE = 16
U_TAIL = 32 - TB * U_LEAD - U_GATE
CONST0 = 48
MASKED = -3e38


class Tally:

    def __init__(self, start=0):
        self.n, self.reg, self.per = start, None, 0

    def add(self, k=1):
        self.n += k
        return self

    def at(self, back=0):
        return self.n - back if self.reg is None else self.reg * self.per + (self.n - back)

    def enter(self, reg, per):
        self.reg, self.per, self.first = reg, per, self.n

    def leave(self, times):
        assert self.n - self.first == self.per, (self.n - self.first, self.per)
        self.n, self.reg = self.first + self.per * times, None


def chain_loop(eng, tally, times, per, body):
    with eng.Fori(0, times) as i:
        tally.enter(i, per)
        body(i)
        tally.leave(times)


def build(nc, A, out):
    with ExitStack() as ctx:
        def sem(name):
            return ctx.enter_context(nc.semaphore(name))

        def allocator(stack):
            return lambda name, shape, dt=F32: stack.enter_context(nc.sbuf_tensor(name, shape, dt))

        sb = allocator(ctx)
        wraw = sb("wraw", [P, R, KB, P])
        whi = sb("whi", [P, R, KB, P], FR)
        wlo = sb("wlo", [P, R, KB, P], FR)
        X = sb("X", [P, KB, S])
        HH = sb("HH", [P, KB, S], FR)
        HL = sb("HL", [P, KB, S], FR)
        T = sb("T", [P, KB, S])
        cols = sb("cols", [P, NCOL])
        mod = sb("mod", [P, 48, 2])
        gsc = sb("gsc", [P, 3, KB])
        ident = sb("ident", [P, P])
        ones = sb("ones", [P, P])
        iota = sb("iota", [P, P])
        eps = sb("eps", [P, 1])
        rr = sb("rr", [P, 2, S])
        rms, rstd = rr[:, 0, :], rr[:, 1, :]
        sc_row = rr[:, :, :].rearrange("p a b -> p (a b)")
        st = sb("st", [P, 24])
        bn = sb("bn", [P, TB, 6])

        m1 = ExitStack()
        a1 = allocator(m1)
        s2 = ExitStack()
        ada1 = allocator(s2)("ada1", [P, 16, D])
        s2.close()
        adaw = a1("adaw", [P, R, D])
        YAH = a1("YAH", [P, 4, S], FR)
        YAL = a1("YAL", [P, 4, S], FR)
        s2 = ExitStack()
        a2 = allocator(s2)
        QT = a2("QT", [P, 4, S])
        KT = a2("KT", [P, 4, S + CTX])
        VV = a2("VV", [P, 6, S])
        s3 = ExitStack()
        a3 = allocator(s3)
        CX = a3("CX", [P, KB, CTX])
        s4 = ExitStack()
        a4 = allocator(s4)
        sc2 = a4("sc2", [P, 2, D])
        junk = a4("junk", [P, 2, D])
        s4.close()
        CH = a3("CH", [P, KB, CTX], FR)
        CL = a3("CL", [P, KB, CTX], FR)
        s3.close()
        s3 = ExitStack()
        a3 = allocator(s3)
        wmask = a3("wmask", [P, HD])
        E = a3("E", [P, 2, 2, WIN])
        PT = a3("PT", [P, 2, 6, P])
        mx = a3("mx", [P, 3, 3])
        s3.close()
        s2.close()
        SS = T[:, :, :].rearrange("p a b -> p (a b)")[:, 0:2304].rearrange("p (u n) -> p u n", u=3)
        s2 = ExitStack()
        a2 = allocator(s2)
        SG = a2("SG", [P, 16, S])
        YBH = a2("YBH", [P, 4, S], FR)
        YBL = a2("YBL", [P, 4, S], FR)
        wsT = a2("wsT", [P, NH, P])
        bsb = a2("bsb", [P, 4, P])
        s2.close()
        UT = T[:, 0:4, :]
        GV = T[:, 4:8, :]
        MX = T[:, 4:8, :]
        m1.close()

        m1 = ExitStack()
        a1 = allocator(m1)
        GS = a1("GS", [P, 2, P, 64])
        actb = a1("actb", [P, 2, S])
        IT = a1("IT", [P, 3, S])
        GH = a1("GH", [P, S], FR)
        s2 = ExitStack()
        a2 = allocator(s2)
        small = a2("small", [P, 16, 16])
        tki = a2("tki", [P, 16, 16], U32)
        tkf = a2("tkf", [P, 16, 16])
        bv = a2("bv", [P, NH, 16])
        bp = a2("bp", [P, NH, 16], U32)
        bab = a2("bab", [P, 2, NH, 16], U32)
        babf = a2("babf", [P, 2, NH, 16])
        sel3 = a2("sel3", [P, 3, P])
        hs = a2("hs", [P, 2, NH])
        s2.close()
        s2 = ExitStack()
        a2 = allocator(s2)
        OI = a2("OI", [P, 8, P], FR)
        OG = a2("OG", [P, 8, 2, P], FR)
        s2.close()
        m1.close()
        QP = GS[:, 0, :, :].rearrange("p a b -> p (a b)").rearrange("p (n t) -> p n t", t=S)
        SC = GS[:, 1, :, :].rearrange("p a b -> p (a b)").rearrange("p (b n k) -> p b n k", b=TB, n=16)
        keysT = T[:, 0:4, :].rearrange("p a b -> p (a b)").rearrange("p (n k) -> p n k", k=P)
        cand = T[:, 0:4, :].rearrange("p a b -> p (a b)").rearrange("p (h a b) -> p h a b", h=NH, a=16)
        SSc = T[:, 4:8, :].rearrange("p a b -> p (a b)").rearrange("p (n k) -> p n k", k=P)
        OJ = T[:, 0:2, :].rearrange("p a b -> p (a b)").rearrange("p (t j) -> p t j", j=P)
        m1 = ExitStack()
        a1 = allocator(m1)
        AJ = a1("AJ", [P, R, S])
        GJ = a1("GJ", [P, R, 8, 64])
        WH = a1("WH", [P, R, S], FR)
        WL = a1("WL", [P, R, S], FR)
        m1.close()

        m1 = ExitStack()
        a1 = allocator(m1)
        ATH = a1("ATH", [P, 4, S], FR)
        ATL = a1("ATL", [P, 4, S], FR)
        OT = a1("OT", [P, 8, S])
        s2 = ExitStack()
        a2 = allocator(s2)
        AQ = a2("AQ", [P, 4, S])
        RQ = a2("RQ", [P, 4, S])
        RK = a2("RK", [P, 4, S])
        RV = a2("RV", [P, 4, D])
        AK = a2("AK", [P, S])
        AV = a2("AV", [P, 4, P])
        AVT = a2("AVT", [P, S])
        s2.close()
        flat = T[:, :, :].rearrange("p a b -> p (a b)")
        AS = flat[:, 768:1536].rearrange("p (u n) -> p u n", u=3)
        APT = flat[:, 1536:2048].rearrange("p (u k q) -> p u k q", u=2, k=2)
        alibi = flat[:, 2048:2304]
        amx = flat[:, 2304:2328].rearrange("p (u c) -> p u c", u=3)
        RSC = T[:, 5:7, :]
        DEC = T[:, 7, :]
        s2 = ExitStack()
        a2 = allocator(s2)
        RH = a2("RH", [P, 8, S], FR)
        RL = a2("RL", [P, 8, S], FR)
        rst4 = a2("rst4", [P, 4, S])
        s2.close()
        m1.close()
        hid = ExitStack()
        a1 = allocator(hid)
        FH = a1("FH", [P, FB, S], FR)
        FL = a1("FL", [P, FB, S], FR)
        hid.close()
        bank = [ctx.enter_context(nc.psum_tensor(f"bank{b}", [P, S], F32)) for b in range(8)]

        act_dram = nc.dram_tensor("act_dram", (P, P, S), F32).ap()
        gate_dram = nc.dram_tensor("gate_dram", (8, P, P, 64), F32).ap()

        w_in = [sem(f"w_in{s}") for s in range(R)]
        w_hi = sem("w_hi")
        w_lo = sem("w_lo")
        tile_done = sem("tile_done")
        tile_evac = sem("tile_evac")
        ada_in = [sem(f"ada_in{s}") for s in range(R)]
        ada1_in = [sem(f"ada1_in{a}") for a in range(16)]
        ada_used = sem("ada_used")
        ada_mul = sem("ada_mul")
        ada_ctx = sem("ada_ctx")
        c_in = sem("c_in")
        c2_in = sem("c2_in")
        const_in = sem("const_in")
        const2_in = sem("const2_in")
        n_eps = sem("n_eps")
        r_pv = sem("r_pv")
        ctx_in = sem("ctx_in")
        late_in = sem("late_in")
        keys_in = sem("keys_in")
        alibi_in = sem("alibi_in")
        dec_in = sem("dec_in")
        bias_in = [sem(f"bias_in{b}") for b in range(2)]
        silu_c = sem("silu_c")
        n_sq = sem("n_sq")
        n_sum = sem("n_sum")
        n_root = sem("n_root")
        n_scaled = sem("n_scaled")
        n_hi = sem("n_hi")
        n_lo = sem("n_lo")
        res_done = sem("res_done")
        gsc_ready = sem("gsc_ready")
        dve = sem("dve_chain")
        at_s = sem("at_s")
        at_masked = sem("at_masked")
        at_exp = sem("at_exp")
        at_p = sem("at_p")
        at_t = sem("at_t")
        at_pt = sem("at_pt")
        at_av = sem("at_av")
        at_hi = sem("at_hi")
        at_lo = sem("at_lo")
        gm_root = sem("gm_root")
        gm_var = sem("gm_var")
        gm_vn = sem("gm_vn")
        gm_mix = sem("gm_mix")
        gm_y = sem("gm_y")
        gm_hi = sem("gm_hi")
        gm_lo = sem("gm_lo")
        mg_m = sem("mg_m")
        mg_hi = sem("mg_hi")
        mg_lo = sem("mg_lo")
        sc_done = sem("sc_done")
        sc_evac = sem("sc_evac")
        tk_diff = sem("tk_diff")
        tk_exp = sem("tk_exp")
        tk_sel = sem("tk_sel")
        tk_tr = sem("tk_tr")
        tk_it = sem("tk_it")
        tk_gate = sem("tk_gate")
        oh_j = sem("oh_j")
        oh_ready = sem("oh_ready")
        oh_low = sem("oh_low")
        g_done = sem("g_done")
        g_high = sem("g_high")
        g_evac = sem("g_evac")
        g_out = [sem(f"g_out{b}") for b in range(2)]
        act_out = [sem(f"act_out{b}") for b in range(2)]
        ag_in = [sem(f"ag_in{s}") for s in range(R)]
        pw = sem("pw")
        pw_hi = sem("pw_hi")
        pw_lo = sem("pw_lo")
        av_turned = sem("av_turned")
        av_ready = sem("av_ready")
        r_s = sem("r_s")
        r_sd = sem("r_sd")
        r_oc = sem("r_oc")
        gn_mu = sem("gn_mu")
        gn_cen = sem("gn_cen")
        gn_sq = sem("gn_sq")
        gn_var = sem("gn_var")
        gn_root = sem("gn_root")
        gn_done = sem("gn_done")
        rg_mul = sem("rg_mul")
        rg_hi = sem("rg_hi")
        rg_lo = sem("rg_lo")
        ff_mul = sem("ff_mul")
        ff_lo = sem("ff_lo")
        out_done = sem("out_done")

        def col(name, k, rows=slice(0, P)):
            a, b = COLS[name]
            return cols[rows, a + k:a + k + 1]

        def bc(ap, axis, n):
            dims = [list(x) for x in ap.ap]
            dims.insert(axis, [0, n])
            return bass.AP(tensor=ap.tensor, offset=ap.offset, ap=dims)

        def evac_before(g):
            return g if g <= G0["V"] else g - COUNT["V"]

        block = ctx.enter_context(nc.Block())

        @block.sync
        def _(sp):
            sp.dma_start(sc2[:, :, :], bass.AP(tensor=A["c"].tensor, offset=0, ap=[[0, P], [D, 2], [1, D]])).then_inc(c_in, 16)
            for dst, src in ((X[:, :, :], A["x"]), (cols[:, :], A["cols"]), (ones[:, :], A["ones"])):
                sp.dma_start(dst, src).then_inc(const_in, 16)
            for a in range(16):
                sp.dma_start(ada1[:, a, :], A["ada"][a, :, :]).then_inc(ada1_in[a], 16)

            def load_ada(a, slot):
                sp.wait_ge(ada_used, a - R + 1)
                sp.dma_start(adaw[:, slot, :], A["ada"][a, :, :]).then_inc(ada_in[slot], 16)

            def load_w(g, slot, peeled=False):
                if not peeled:
                    sp.wait_ge(w_lo, g - R + 1)
                sp.dma_start(wraw[:, slot, :, :].rearrange("p k c -> p (k c)"), A["w"][g, :, :])\
                    .then_inc(w_in[slot], 16)

            sp.dma_start(CX[:, :, :], A["ctx"]).then_inc(ctx_in, 16)
            for dst, src in ((ident[:, :], A["ident"]), (iota[:, :], A["iota"])):
                sp.dma_start(dst, src).then_inc(const2_in, 16)
            for g in range(R):
                load_w(g, g, peeled=True)
            with sp.Fori(0, 3) as i:
                for u in range(4):
                    load_w(i * 4 + (4 + u), u)
            for a in range(16, 20):
                load_ada(a, a % R)
            for g in range(16, 20):
                load_w(g, g % R)
            load_ada(20, 0)
            load_ada(21, 1)
            with sp.Fori(0, 3) as i:
                for u in range(4):
                    load_w(i * 4 + (20 + u), u)
                    for k in range(2):
                        load_ada(i * 8 + (22 + 2 * u + k), (22 + 2 * u + k) % R)
            load_w(32, 0)
            load_ada(46, 2)
            load_ada(47, 3)
            for g in range(33, G0["pa"]):
                load_w(g, g % R)
            n = (G0["U"] - G0["pa"]) // 4 + TB * U_LEAD
            with sp.Fori(0, n) as i:
                for u in range(4):
                    load_w(i * 4 + (G0["pa"] + u), u)
            gu0 = G0["U"] + 4 * TB * U_LEAD

            def store_g(b, buf):
                sp.wait_ge(g_evac, b * 16 + 16)
                sp.dma_start(gate_dram[b, :, :, :].rearrange("i j t -> i (j t)"),
                             GS[:, buf, :, :].rearrange("p j t -> p (j t)")).then_inc(g_out[buf], 16)

            for u in range(16):
                load_w(gu0 + u, u % R)
            store_g(0, 0)
            with sp.Fori(0, 3) as i:
                for half in range(2):
                    for u in range(8):
                        load_w(i * 16 + (gu0 + 16 + 8 * half + u), u % R)
                    store_g(i * 2 + (1 + half), (1 + half) % 2)
            gt0 = gu0 + 4 * U_GATE
            for u in range(8):
                load_w(gt0 + u, u % R)
            store_g(7, 1)
            with sp.Fori(0, U_TAIL - 2) as i:
                for u in range(4):
                    load_w(i * 4 + (gt0 + 8 + u), u)

            def load_ag(j, slot, peeled=False):
                if not peeled:
                    sp.wait_ge(pw_lo, j - R + 1)
                sp.dma_start(AJ[:, slot, :], act_dram[j, :, :]).then_inc(ag_in[slot], 16)
                sp.dma_start(GJ[:, slot, :, :], gate_dram[:, :, j, :].rearrange("b i t -> i b t"))\
                    .then_inc(ag_in[slot], 16)

            for b in range(2):
                sp.wait_ge(g_out[b], 64)
            for u in range(R):
                sp.wait_ge(act_out[u % 2], 16 * (u // 2 + 1))
                load_ag(u, u, peeled=True)
            for u in range(R):
                load_w(G0["V"] + u, u)
            for b in range(2):
                sp.wait_ge(act_out[b], 16 * 64)
            with sp.Fori(0, 31) as i:
                for u in range(R):
                    load_w(i * 4 + (G0["V"] + 4 + u), u)
                    load_ag(i * 4 + (4 + u), u)
            n = (NT - G0["aq"]) // 4
            with sp.Fori(0, n) as i:
                for u in range(4):
                    load_w(i * 4 + (G0["aq"] + u), u)
            for kb in range(KB):
                sp.wait_ge(n_scaled, 6 * KB + kb + 1)
                sp.dma_start(out[:, kb, :], T[:, kb, :]).then_inc(out_done, 16)
            sp.wait_ge(out_done, 16 * KB)

        @block.gpsimd
        def _(pool):
            def lo(g, slot):
                pool.wait_ge(w_hi, g + 1)
                nc.gpsimd.tensor_tensor(wlo[:, slot, :, :].rearrange("p k c -> p (k c)"),
                                        wraw[:, slot, :, :].rearrange("p k c -> p (k c)"),
                                        whi[:, slot, :, :].rearrange("p k c -> p (k c)").bitcast(F32),
                                        ALU.subtract).then_inc(w_lo, 1)

            def los(g0, n):
                while n and g0 % R:
                    lo(g0, g0 % R)
                    g0, n = g0 + 1, n - 1
                if n >= 8:
                    with pool.Fori(0, n // 4) as i:
                        for u in range(4):
                            lo(i * 4 + (g0 + u), u)
                    g0, n = g0 + n // 4 * 4, n % 4
                for u in range(n):
                    lo(g0 + u, (g0 + u) % R)

            pool.wait_ge(silu_c, 1)
            for a in range(KB):
                pool.wait_ge(ada_used, a + 1)
                nc.gpsimd.tensor_tensor(ada1[:, a, :], ada1[:, a, :], sc2[:, 1, :], ALU.mult).then_inc(ada_mul, 1)

            def bias(pair):
                b = pair % 2
                for hh in range(2):
                    for r in range(2):
                        L = 15 * 127
                        skewed = bass.AP(tensor=A["rpb"].tensor, offset=(2 * pair + hh) * L + (1 - r) * 127 + 63,
                                         ap=[[8 * L - 1, 64], [127, 14], [1, 64]])
                        pool.dma_start(E[64 * r:64 * r + 64, b, hh, :].rearrange("p (m k) -> p m k", k=64), skewed)\
                            .then_inc(bias_in[b], 16)

            los(0, 6)
            pool.wait_ge(n_lo, 2 * KB)
            pool.dma_start(wmask[:, :], A["wmask"]).then_inc(late_in, 16)
            bias(0)
            pool.dma_start(sc_row, bass.AP(tensor=A["c"].tensor, offset=0, ap=[[0, P], [1, D]])).then_inc(c2_in, 16)
            los(6, 9)
            pool.wait_ge(tile_done, G0["gu"])
            bias(1)
            for pair in range(2, 4):
                pool.wait_ge(at_masked, 8 * (pair - 1))
                bias(pair)
            los(15, G0["gates"] - 15)
            pool.wait_ge(at_lo, 32)
            pool.dma_start(wsT[:, :, :], A["wsT"]).then_inc(late_in, 16)
            pool.dma_start(bsb[:, :, :], A["bs"]).then_inc(late_in, 16)
            los(G0["gates"], G0["wq"] - G0["gates"] + 3)
            pool.wait_ge(n_lo, 3 * KB)
            pool.dma_start(keysT, A["keys"]).then_inc(keys_in, 16)
            los(G0["wq"] + 3, 17)
            gu0 = G0["U"] + 4 * TB * U_LEAD
            los(G0["U"] + 4, gu0 + 3 - (G0["U"] + 4))
            with pool.Fori(0, U_GATE) as i:
                for u in range(4):
                    for half in range(2):
                        q = i * 8 + (2 * u + half)
                        pool.wait_ge(oh_j, q + 1)
                        nc.gpsimd.tensor_tensor(OG[:, 4 * half:4 * half + 4, 1, :], OJ[:, 4 * half:4 * half + 4, :],
                                                bc(IT[:, 2, bass.ds(q * 4, 4)], 2, P), ALU.mult).then_inc(oh_low, 1)
                    lo(i * 4 + (gu0 + 3 + u), (gu0 + 3 + u) % R)
            los(gu0 + 3 + 4 * U_GATE, G0["rg"] + 3 - (gu0 + 3 + 4 * U_GATE))
            pool.wait_ge(tile_evac, evac_before(G0["rg"]))
            pool.dma_start(alibi, A["alibi"]).then_inc(alibi_in, 16)
            for h in range(4):
                if h:
                    pool.wait_ge(r_sd, 4 * h)
                pool.dma_start(DEC, A["dec"][h, :, :]).then_inc(dec_in, 16)
            los(G0["rg"] + 3, NT - G0["rg"] - 3)

        @block.scalar
        def _(act):
            def hi(g, slot, turns, peeled=False):
                act.wait_ge(w_in[slot], turns)
                if not peeled:
                    act.wait_ge(tile_done, g - R + 1)
                nc.scalar.activation(whi[:, slot, :, :].rearrange("p k c -> p (k c)"),
                                     wraw[:, slot, :, :].rearrange("p k c -> p (k c)"), ACT.Copy).then_inc(w_hi, 1)

            def ahead(g0, u, i=None):
                t = g0 + u + 3
                if i is None:
                    if t < NT:
                        hi(t, t % R, 16 * (t // R + 1), peeled=t < R)
                else:
                    hi(i * 4 + t, t % R, i * 16 + 16 * (t // R + 1))

            def tile_ready(g):
                act.wait_ge(tile_done, g + 1)

            norms = [0]
            done_blocks = [0]

            def norm_squares(src, width, ready=None, block_ready=None):
                for kb in range(KB):
                    if kb == 0 and ready:
                        for s_, v_ in ready:
                            act.wait_ge(s_, v_)
                    if block_ready:
                        act.wait_ge(block_ready[0], block_ready[1] + kb + 1)
                    nc.scalar.activation(T[:, kb, 0:width], src[:, kb, :], ACT.Square).then_inc(n_sq, 1)

            def norm_root(width, b=4):
                norms[0] += 1
                act.wait_ge(n_sum, norms[0])
                nc.scalar.activation(rms[:, 0:width], bank[b][:, 0:width], ACT.Sqrt, bias=eps[:, 0:1], scale=1.0 / D)\
                    .then_inc(n_root, 1)

            def norm_apply(width, shift, H):
                for kb in range(KB):
                    done_blocks[0] += 1
                    act.wait_ge(n_scaled, done_blocks[0])
                    kw = {} if shift is None else {"bias": shift(kb)}
                    nc.scalar.activation(H[:, kb, :], T[:, kb, 0:width], ACT.Identity, **kw).then_inc(n_hi, 1)

            act.wait_ge(c_in, 16)
            nc.scalar.activation(sc2[:, :, :], sc2[:, :, :], ACT.Silu).then_inc(silu_c, 1)
            act.wait_ge(const_in, CONST0)
            norm_squares(X, S)
            act.wait_ge(n_eps, 1)
            norm_root(S)
            for g in range(3):
                ahead(-3, g)
            act.wait_ge(gsc_ready, 1)
            norm_apply(S, lambda kb: mod[:, kb, 0:1], HH)
            ahead(0, 0)
            norm_squares(CX, CTX, ready=[(n_lo, KB), (ctx_in, 16)])
            ahead(1, 0)
            for a in range(KB):
                act.wait_ge(ada_mul, a + 1)
                nc.scalar.activation(ada1[:, a, :], ada1[:, a, :], ACT.Copy, accum_out=mod[:, a, 1:2])\
                    .then_inc(ada_ctx, 1)
            norm_root(CTX)
            ahead(2, 0)
            act.wait_ge(gsc_ready, 2)
            norm_apply(CTX, lambda kb: mod[:, kb, 1:2], CH)
            for g in range(3, 12):
                ahead(g, 0)
            act.wait_ge(c2_in, 16)
            nc.scalar.activation(sc_row, sc_row, ACT.Silu).then_inc(silu_c, 1)

            def at1_evac(n, it):
                act.wait_ge(at_t, it * 16 + (n + 1))
                if n >= 2:
                    act.wait_ge(at_av, it * 16 + (n - 1))
                b = n % 2
                nc.scalar.activation(PT[:, b, 0:4, :].rearrange("p k q -> p (k q)"), bank[2 * b][:, :], ACT.Copy)\
                    .then_inc(at_pt, 1)
                nc.scalar.activation(PT[:, b, 4:6, :].rearrange("p k q -> p (k q)"), bank[2 * b + 1][:, 0:256],
                                     ACT.Copy).then_inc(at_pt, 1)

            def at1_hi(n, it):
                act.wait_ge(at_av, it * 16 + (n + 1))
                pair, hh, a = n // 8, n // 4 % 2, n % 4
                r = slice(64 * hh, 64 * hh + 64)
                nc.scalar.activation(YAH[r, bass.ds(it * 2 + pair, 1), a * P:(a + 1) * P]
                                     .rearrange("p o q -> p (o q)"),
                                     bank[2 * (n % 2) + 1][r, 256:384], ACT.Copy).then_inc(at_hi, 1)

            with act.Fori(0, 2) as it:
                for n in range(16 + 3):
                    if n >= 3:
                        at1_hi(n - 3, it)
                    if n < 16:
                        act.wait_ge(at_masked, it * 16 + (n + 1))
                        nc.scalar.activation(SS[:, n % 3, :], SS[:, n % 3, :], ACT.Exp, bias=mx[:, n % 3, 0:1],
                                             accum_out=mx[:, n % 3, 1:2]).then_inc(at_exp, 1)
                    if 2 <= n < 18:
                        at1_evac(n - 2, it)

            for u in range(4):
                ahead(G0["gu"], u)
                tile_ready(G0["gu"] + u)
                if u == 0:
                    act.wait_ge(at_lo, 32)
                nc.scalar.activation(UT[:, u, :], bank[u][:, :], ACT.Gelu_apprx_tanh).then_inc(tile_evac, 1)
            for u in range(4):
                ahead(G0["gv"], u)
            tile_ready(G0["gv"] + 3)
            for b in (3, 2, 1, 0):
                nc.scalar.activation(GV[:, b, :], bank[4 + b][:, :], ACT.Gelu_apprx_tanh).then_inc(tile_evac, 1)
            act.wait_ge(gm_var, 4)
            nc.scalar.activation(st[:, 8:12], st[:, 4:8], ACT.Sqrt, bias=eps[:, 0:1]).then_inc(gm_root, 1)
            with act.Fori(0, 4) as i:
                for u in range(4):
                    ahead(G0["gates"], u, i)
                    tile_ready(i * 4 + (G0["gates"] + u))
                    nc.scalar.activation(SG[:, bass.ds(i * 4 + u, 1), :].rearrange("p o t -> p (o t)"),
                                         bank[u][:, :], ACT.Sigmoid).then_inc(tile_evac, 1)
            for b in range(4):
                act.wait_ge(gm_y, b + 1)
                nc.scalar.activation(YBH[:, b, :], MX[:, b, :], ACT.Copy).then_inc(gm_hi, 1)
            for u in range(8):
                ahead(G0["pa"], u)
                if u >= 4:
                    for k in range(2):
                        kb = 2 * (u - 4) + k
                        act.wait_ge(mg_m, kb + 1)
                        nc.scalar.activation(HH[:, kb, :], T[:, kb, :], ACT.Copy).then_inc(mg_hi, 1)
            for u in range(8):
                ahead(G0["out"], u)
            norm_squares(X, S, ready=[(mg_lo, KB)], block_ready=(tile_evac, G0["out"]))
            norm_root(S)
            norm_apply(S, lambda kb: mod[:, 24 + kb, 0:1], HH)
            with act.Fori(0, 4) as i:
                for u in range(4):
                    ahead(G0["wq"], u, i)
                    tile_ready(i * 4 + (G0["wq"] + u))
                    nc.scalar.activation(QP[:, bass.ds(i * 4 + u, 1), :].rearrange("p o t -> p (o t)"),
                                         bank[u][:, :], ACT.Copy).then_inc(tile_evac, 1)
            for n in range(16):
                act.wait_ge(sc_done, n + 1)
                nc.scalar.activation(SC[:, n // 4, 4 * (n % 4):4 * (n % 4) + 4, :].rearrange("p n k -> p (n k)"),
                                     bank[4 + n % 4][:, :], ACT.Copy).then_inc(sc_evac, 1)

            def act_tile(j, u, evac_turns=None):
                tile_ready(j + G0["U"])
                if evac_turns is not None:
                    act.wait_ge(act_out[u % 2], evac_turns)
                nc.scalar.activation(actb[:, u % 2, :], bank[u][:, :], ACT.Gelu_apprx_tanh).then_inc(tile_evac, 1)
                act.wait_ge(tile_evac, j + (G0["U"] + 1))
                act.dma_start(act_dram[j, :, :], actb[:, u % 2, :]).then_inc(act_out[u % 2], 16)

            def u_iteration(i):
                for u in range(4):
                    ahead(G0["U"], u, i)
                    act_tile(i * 4 + u, u, i * 32 + 16 * (u // 2))

            for tb in range(TB):
                if tb == 0:
                    for u in range(4):
                        ahead(G0["U"], u)
                        act_tile(u, u, 16 * (u // 2) if u >= 2 else None)
                    u_iteration(1)
                else:
                    with act.Fori(0, U_LEAD - 1) as i:
                        u_iteration(i + U_LEAD * tb)
                act.wait_ge(tk_diff, tb + 1)
                nc.scalar.activation(bv[:, :, :], bv[:, :, :], ACT.Exp).then_inc(tk_exp, 1)
                u_iteration(U_LEAD * tb + U_LEAD - 1)

            def g_group(q, m, stored=None):
                act.wait_ge(g_done, q + 1)
                if stored is not None:
                    act.wait_ge(g_out[m // 16], stored)
                for k in range(2):
                    t = 4 * (m % 16) + 2 * k
                    nc.scalar.activation(GS[:, m // 16, :, t:t + 2],
                                         bank[4 + 2 * (m % 2) + k][:, :].rearrange("p (t w j) -> p w j t", t=2, w=2)[:, 0],
                                         ACT.Copy).then_inc(g_high, 1)

            def gate_blocks(i, first):
                for k in range(4):
                    it = i * 4 + (TB * U_LEAD + k)
                    for u in range(4):
                        ahead(G0["U"], u, it)
                        act_tile(it * 4 + u, u, it * 32 + 16 * (u // 2))
                        for e in range(2):
                            m = 8 * k + 2 * u + e
                            g_group(i * 32 + m, m, i * 16 if m % 16 == 0 and not first else None)

            gate_blocks(0, True)
            with act.Fori(1, 4) as i:
                gate_blocks(i, False)
            with act.Fori(TB * U_LEAD + U_GATE, 32) as i:
                u_iteration(i)

            def pw_tile(j, slot):
                act.wait_ge(pw, j + 1)
                nc.scalar.activation(WH[:, slot, :], AJ[:, slot, :], ACT.Copy).then_inc(pw_hi, 1)

            for u in range(4):
                pw_tile(u, u)
                ahead(G0["V"], u)
            with act.Fori(1, 32) as i:
                for u in range(4):
                    pw_tile(i * 4 + u, u)
                    ahead(G0["V"], u, i)

            norm_squares(X, S, block_ready=(res_done, 0))
            norm_root(S, 0)
            for kb in range(KB):
                done_blocks[0] += 1
                act.wait_ge(n_scaled, done_blocks[0])
                nc.scalar.activation(T[:, kb, :], X[:, kb, :], ACT.Square).then_inc(n_sq, 1)
            norm_root(S)
            norm_apply(S, None, HH)
            for g in range(G0["aq"], G0["rg"]):
                ahead(g, 0)

            def at2_evac(n, it):
                act.wait_ge(at_t, it * 16 + (32 + n + 1))
                if n >= 2:
                    act.wait_ge(at_av, it * 16 + (32 + n - 1))
                b = n % 2
                nc.scalar.activation(APT[:, b, :, :].rearrange("p k q -> p (k q)"), bank[b][:, 0:256], ACT.Copy)\
                    .then_inc(at_pt, 1)

            def at2_hi(n, it):
                act.wait_ge(at_av, it * 16 + (32 + n + 1))
                m, r, a = n // 8, n // 4 % 2, n % 4
                rr = slice(64 * r, 64 * r + 64)
                nc.scalar.activation(ATH[rr, bass.ds(it * 2 + m, 1), a * P:(a + 1) * P]
                                     .rearrange("p o q -> p (o q)"),
                                     bank[n % 2][rr, 256:384], ACT.Copy).then_inc(at_hi, 1)

            def at2_sink(n, it):
                act.wait_ge(at_masked, it * 16 + (32 + n + 1))
                m, r = n // 8, n // 4 % 2
                nc.scalar.activation(amx[:, n % 3, 3:4], amx[:, n % 3, 2:3], ACT.Exp).then_inc(at_exp, 1)

            with act.Fori(0, 2) as it:
                for n in range(16 + 3):
                    if n >= 3:
                        at2_hi(n - 3, it)
                    if n < 16:
                        at2_sink(n, it)
                        nc.scalar.activation(AS[:, n % 3, :], AS[:, n % 3, :], ACT.Exp, bias=amx[:, n % 3, 0:1],
                                             accum_out=amx[:, n % 3, 1:2]).then_inc(at_exp, 1)
                    if 2 <= n < 18:
                        at2_evac(n - 2, it)
            for k in range(8):
                act.wait_ge(gn_cen, k + 1)
                if k == 0:
                    act.wait_ge(at_lo, 64)
                    act.wait_ge(r_pv, 16)
                nc.scalar.activation(T[:, k, :], OT[:, k, :], ACT.Square).then_inc(gn_sq, 1)
            for h in range(4):
                act.wait_ge(gn_var, h + 1)
                nc.scalar.activation(rst4[:, h, :], bank[4 + h][:, :], ACT.Sqrt, bias=eps[:, 0:1], scale=1.0 / 256)\
                    .then_inc(gn_root, 1)
            for k in range(8):
                ahead(G0["rg"], k)
                tile_ready(G0["rg"] + k)
                nc.scalar.activation(T[:, k, :], bank[(G0["rg"] + k) % R][:, :], ACT.Silu).then_inc(tile_evac, 1)
                act.wait_ge(rg_mul, k + 1)
                nc.scalar.activation(RH[:, k, :], T[:, k, :], ACT.Copy).then_inc(rg_hi, 1)
            for k in range(8):
                ahead(G0["ga2"], k)
                tile_ready(G0["ga2"] + k)
                act.wait_ge(rg_lo, k + 1)
                nc.scalar.activation(T[:, k, :], bank[(G0["ga2"] + k) % R][:, :], ACT.Sigmoid).then_inc(tile_evac, 1)
            for k in range(4):
                ahead(G0["atto"], k)
            for k in range(8):
                ahead(G0["gr2"], k)
                tile_ready(G0["gr2"] + k)
                if k == 0:
                    act.wait_ge(tile_evac, evac_before(G0["gr2"]))
                nc.scalar.activation(OT[:, k, :], bank[(G0["gr2"] + k) % R][:, :], ACT.Sigmoid).then_inc(tile_evac, 1)
            for k in range(8):
                ahead(G0["reto"], k)
                act.wait_ge(mg_m, KB + k + 1)
                if k == 0:
                    act.wait_ge(tile_done, G0["reto"])
                nc.scalar.activation(HH[:, k, :], T[:, k, :], ACT.Copy).then_inc(mg_hi, 1)
            for k in range(8):
                ahead(G0["out2"], k)
            norm_squares(X, S, ready=[(mg_lo, 2 * KB)],
                         block_ready=(tile_evac, evac_before(G0["out2"])))
            norm_root(S)
            norm_apply(S, None, HH)
            def ffn_body(i, peeled):
                for u in range(4):
                    g = i * 4 + (G0["gateup"] + u)
                    ahead(G0["gateup"], u, i)
                    if u % 2 == 0:
                        tile_ready(g)
                        if not peeled:
                            act.wait_ge(ff_lo, i * 2 + (u // 2 - 1))
                        nc.scalar.activation(T[:, u // 2, :], bank[(G0["gateup"] + u) % R][:, :], ACT.Silu)\
                            .then_inc(tile_evac, 1)
                    else:
                        act.wait_ge(ff_mul, i * 2 + (u // 2 + 1))
                        nc.scalar.activation(FH[:, bass.ds(i * 2 + u // 2, 1), :].rearrange("p o t -> p (o t)"),
                                             T[:, u // 2, :], ACT.Copy).then_inc(tile_evac, 1)

            ffn_body(0, True)
            with act.Fori(1, FB // 2) as i:
                ffn_body(i, False)
            for k in range(FB):
                ahead(G0["down"], k)
            norm_squares(X, S, block_ready=(res_done, KB))
            norm_root(S, 0)

        @block.tensor
        def _(pe):
            def three(out_, ah, al, bh, bl, first, last, **kw):
                pe.matmul(out_, ah, bh, start=first, stop=False, **kw)
                pe.matmul(out_, ah, bl, start=False, stop=False, **kw)
                return pe.matmul(out_, al, bh, start=False, stop=last, **kw)

            def tile_wait(g, e):
                pe.wait_ge(w_lo, g + 1)
                pe.wait_ge(tile_evac, e - R + 1)

            def columns(g, slot, e, xh=HH, xl=HL, first=False, split=None):
                if first:
                    pe.wait_ge(w_lo, g + 1)
                else:
                    tile_wait(g, e)
                for kb in range(KB):
                    if split:
                        pe.wait_ge(split[0], split[1] + kb + 1)
                    mm = three(bank[slot][:, :], whi[:, slot, kb, :], wlo[:, slot, kb, :], xh[:, kb, :], xl[:, kb, :],
                               kb == 0, kb == KB - 1)
                return mm

            def rows(b0, slot, part, xh, xl, blocks):
                wh = whi[:, slot, :, :].rearrange("p k c -> p (k c)")
                wl = wlo[:, slot, :, :].rearrange("p k c -> p (k c)")
                for b in range(blocks):
                    for k in range(2):
                        x = (slice(0, P), 2 * part + k, slice(b * P, (b + 1) * P))
                        w = (slice(0, P), slice(k * S, (k + 1) * S))
                        mm = three(bank[b0 + b][:, :], xh[x], xl[x], wh[w], wl[w], part == 0 and k == 0,
                                   part == 3 and k == 1)
                return mm

            blocks = [0]

            def norm_sum(width, b=4):
                for kb in range(KB):
                    blocks[0] += 1
                    pe.wait_ge(n_sq, blocks[0])
                    mm = pe.matmul(bank[b][:, 0:width], ones[:, :], T[:, kb, 0:width], start=(kb == 0),
                                   stop=(kb == KB - 1))
                mm.then_inc(n_sum, 1)

            pe.wait_ge(const_in, CONST0)
            norm_sum(S)
            for u in range(4):
                if u == 2:
                    norm_sum(CTX)
                columns(G0["q"] + u, u, 0, first=True, split=(n_lo, 0) if u == 0 else None).then_inc(tile_done, 1)
            pe.wait_ge(n_lo, 2 * KB)
            for u in range(4):
                columns(G0["k"] + u, u, G0["k"] + u)
                for kb in range(KB):
                    mm = three(bank[4 + u][:, 0:CTX], whi[:, u, kb, :], wlo[:, u, kb, :], CH[:, kb, :], CL[:, kb, :],
                               kb == 0, kb == KB - 1)
                mm.then_inc(tile_done, 1)
            pe.wait_ge(tile_evac, G0["v"])
            for u in range(4):
                pe.wait_ge(w_lo, G0["v"] + u + 1)
                rows(0, u, u, HH, HL, TB)
                rows(4, u, u, CH, CL, 2).then_inc(tile_done, 1)

            pe.wait_ge(const2_in, 32)
            pe.wait_ge(tile_evac, G0["gu"])

            def at1_scores(n, it):
                pair, hh, a = n // 8, n // 4 % 2, n % 4
                b = n % 2
                if n >= 2:
                    pe.wait_ge(at_masked, it * 16 + (n - 1))
                r = slice(64 * hh, 64 * hh + 64)
                q = QT[r, 2 * it + pair, a * P:(a + 1) * P]
                k = KT[r, 2 * it + pair, :]
                pe.matmul(bank[4 + 2 * b][:, :], q, k[:, 0:S], start=True, stop=True)
                pe.matmul(bank[5 + 2 * b][:, 0:CTX], q, k[:, S:S + CTX], start=True, stop=True).then_inc(at_s, 1)

            def at1_turn(n, it):
                b = n % 2
                pe.wait_ge(at_p, it * 16 + (n + 1))
                if n >= 2:
                    pe.wait_ge(at_pt, it * 32 + 2 * (n - 1))
                    pe.wait_ge(at_lo, it * 16 + (n - 1))
                for k in range(6):
                    o = bank[2 * b + k // 4][:, (k % 4) * P:(k % 4 + 1) * P]
                    mm = pe.transpose(o, SS[:, n % 3, k * P:(k + 1) * P], ident[:, :])
                mm.then_inc(at_t, 1)

            def at1_values(n, it):
                pair, hh = n // 8, n // 4 % 2
                b = n % 2
                pe.wait_ge(at_pt, it * 32 + 2 * (n + 1))
                for k in range(6):
                    mm = pe.matmul(bank[2 * b + 1][64 * hh:64 * hh + 64, 256:384],
                                   VV[:, k, (4 * it + 2 * pair + hh) * HD:(4 * it + 2 * pair + hh + 1) * HD], PT[:, b, k, :], start=(k == 0), stop=(k == 5))
                mm.then_inc(at_av, 1)

            for it in range(2):
                for n in range(16 + 3):
                    if n < 16:
                        at1_scores(n, it)
                    if 2 <= n < 18:
                        at1_turn(n - 2, it)
                    if n >= 3:
                        at1_values(n - 3, it)

            pe.wait_ge(at_lo, 32)
            for u in range(4):
                columns(G0["gu"] + u, u, G0["gu"] + u).then_inc(tile_done, 1)
            for u in range(4):
                pe.wait_ge(w_lo, G0["gv"] + u + 1)
                rows(4, u, u, HH, HL, TB).then_inc(tile_done, 1)
            with pe.Fori(0, 4) as i:
                for u in range(4):
                    g = i * 4 + (G0["gates"] + u)
                    columns(g, u, g).then_inc(tile_done, 1)
            pe.wait_ge(gm_vn, 4)
            pe.wait_ge(late_in, 48)
            for g in range(NH):
                for tb in range(TB):
                    mm = pe.matmul(bank[4 + g // 2][64 * (g % 2):64 * (g % 2) + 64, tb * P:(tb + 1) * P],
                                   GV[:, tb, 64 * g:64 * g + 64], wsT[:, g, :], start=True, stop=True)
            mm.then_inc(gm_mix, 1)

            def narrow(g, slot, e, xh, xl):
                tile_wait(g, e)
                for half in range(2):
                    for kb in range(4):
                        k = 4 * half + kb
                        mm = three(bank[slot + 4 * half][:, :], whi[:, slot, k, :], wlo[:, slot, k, :], xh[:, kb, :],
                                   xl[:, kb, :], kb == 0, kb == 3)
                mm.then_inc(tile_done, 1)

            pe.wait_ge(at_lo, 32)
            pe.wait_ge(gm_y, 4)
            for u in range(4):
                narrow(G0["pa"] + u, u, G0["pa"] + u, YAH, YAL)
            pe.wait_ge(gm_lo, 4)
            for u in range(4):
                narrow(G0["pb"] + u, u, G0["pb"] + u, YBH, YBL)
            def layer(name, split, e0=0, xh=HH, xl=HL):
                for u in range(4):
                    g = G0[name] + u
                    columns(g, g % R, g - e0, xh, xl, split=split if u == 0 else None).then_inc(tile_done, 1)
                if COUNT[name] > 4:
                    with pe.Fori(1, COUNT[name] // 4) as i:
                        for u in range(4):
                            t = G0[name] + u
                            columns(i * 4 + t, t % R, i * 4 + (t - e0), xh, xl).then_inc(tile_done, 1)

            layer("out", (mg_lo, 0))
            norm_sum(S)
            layer("wq", (n_lo, 2 * KB))
            pe.wait_ge(tile_evac, G0["U"])
            pe.wait_ge(keys_in, 16)
            for n in range(16):
                tb, quad = n // 4, n % 4
                if n >= 4:
                    pe.wait_ge(sc_evac, n - 3)
                for k in range(4):
                    hp = 4 * quad + k
                    mm = pe.matmul(bank[4 + quad][:, k * P:(k + 1) * P], QP[:, hp, tb * P:(tb + 1) * P],
                                   keysT[:, hp, :], start=True, stop=True)
                mm.then_inc(sc_done, 1)

            def u_tile(g, slot):
                columns(g, slot, g).then_inc(tile_done, 1)

            for tb in range(TB):
                with pe.Fori(0, U_LEAD) as i:
                    for u in range(4):
                        u_tile(i * 4 + (G0["U"] + 4 * U_LEAD * tb + u), u)
                pe.wait_ge(tk_sel, tb + 1)
                if tb == 0:
                    pe.wait_ge(sc_evac, 16)
                else:
                    pe.wait_ge(tk_it, tb)
                for k in range(3):
                    mm = pe.transpose(bank[4][:, k * P:(k + 1) * P], sel3[:, k, :], ident[:, :])
                mm.then_inc(tk_tr, 1)
            pe.wait_ge(tk_it, TB)

            def gate_group(q, half, peeled=False):
                pe.wait_ge(oh_ready, q + 1)
                pe.wait_ge(oh_low, q + 1)
                if not peeled:
                    pe.wait_ge(g_evac, q - 1)
                for e in range(4):
                    t = 4 * half + e
                    mm = pe.matmul(bank[4 + 2 * half + e // 2][:, e % 2 * 256:e % 2 * 256 + 256], OI[:, t, :],
                                   OG[:, t, :, :].rearrange("p w j -> p (w j)"), start=True, stop=True)
                mm.then_inc(g_done, 1)

            gu0 = G0["U"] + 4 * TB * U_LEAD
            for u in range(4):
                u_tile(gu0 + u, u)
                for k in range(2):
                    gate_group(2 * u + k, k, peeled=(u == 0))
            with pe.Fori(1, U_GATE) as i:
                for u in range(4):
                    u_tile(i * 4 + (gu0 + u), u)
                    for k in range(2):
                        gate_group(i * 8 + (2 * u + k), k)
            with pe.Fori(0, U_TAIL) as i:
                for u in range(4):
                    u_tile(i * 4 + (gu0 + 4 * U_GATE + u), u)

            def add_up(slot, xh, xl, first, last):
                for kb in range(KB):
                    mm = three(bank[kb][:, :], whi[:, slot, kb, :], wlo[:, slot, kb, :], xh, xl, first, last)
                mm.then_inc(tile_done, 1)

            def v_tile(j, u, first=False, last=False):
                pe.wait_ge(w_lo, j + (G0["V"] + 1))
                pe.wait_ge(pw_lo, j + 1)
                add_up(u, WH[:, u, :], WL[:, u, :], first, last)

            pe.wait_ge(tile_evac, G0["V"])
            pe.wait_ge(g_evac, P)
            for u in range(4):
                v_tile(u, u, first=(u == 0))
            with pe.Fori(1, 31) as i:
                for u in range(4):
                    v_tile(i * 4 + u, u)
            for u in range(4):
                v_tile(124 + u, u, last=(u == 3))

            norm_sum(S, 0)
            norm_sum(S)
            e0 = COUNT["V"]
            layer("aq", (n_lo, 3 * KB), e0)
            with pe.Fori(1, 3) as i:
                for u in range(4):
                    g = i * 4 + (G0["aq"] + u)
                    columns(g, u, g - e0).then_inc(tile_done, 1)
            for h in range(2):
                if h:
                    pe.wait_ge(tile_evac, evac_before(G0["rv"]))
                for u in range(4):
                    pe.wait_ge(w_lo, G0["rv"] + 4 * h + u + 1)
                    rows(4 - 4 * h, u, u, HH, HL, TB).then_inc(tile_done, 1)
            columns(G0["av"], 0, G0["av"] - e0).then_inc(tile_done, 1)
            columns(G0["ak"], 1, G0["ak"] - e0).then_inc(tile_done, 1)
            pe.wait_ge(tile_evac, evac_before(G0["av"]) + 1)
            for b in range(TB):
                mm = pe.transpose(bank[7][:, b * P:(b + 1) * P], AVT[:, b * P:(b + 1) * P], ident[:, :])
            mm.then_inc(av_turned, 1)
            pe.wait_ge(av_ready, 1)

            pe.wait_ge(tile_evac, evac_before(G0["rg"]))

            def at2_scores(n, it):
                m, r, a = n // 8, n // 4 % 2, n % 4
                b = n % 2
                if n >= 2:
                    pe.wait_ge(at_masked, it * 16 + (32 + n - 1))
                rr = slice(64 * r, 64 * r + 64)
                k0, k1 = (a - 1) * P if a else 0, (a + 1) * P
                pe.matmul(bank[4 + b][:, 256 - (k1 - k0):256], AQ[rr, 2 * it + m, a * P:(a + 1) * P], AK[rr, k0:k1],
                          start=True, stop=True).then_inc(at_s, 1)

            def at2_turn(n, it):
                b = n % 2
                pe.wait_ge(at_p, it * 16 + (32 + n + 1))
                if n >= 2:
                    pe.wait_ge(at_pt, it * 16 + (64 + n - 1))
                    pe.wait_ge(at_lo, it * 16 + (32 + n - 1))
                for k in range(2):
                    mm = pe.transpose(bank[b][:, k * P:(k + 1) * P], AS[:, n % 3, k * P:(k + 1) * P], ident[:, :])
                mm.then_inc(at_t, 1)

            def at2_values(n, it):
                r, a = n // 4 % 2, n % 4
                b = n % 2
                pe.wait_ge(at_pt, it * 16 + (64 + n + 1))
                for k in range(2):
                    kb = max(a - 1 + k, 0)
                    mm = pe.matmul(bank[b][64 * r:64 * r + 64, 256:384], AV[:, kb, 64 * r:64 * r + 64],
                                   APT[:, b, k, :], start=(k == 0), stop=(k == 1))
                mm.then_inc(at_av, 1)

            def ret_step(h, J):
                if J < TB:
                    n = 4 * h + J
                    if n >= 2:
                        pe.wait_ge(r_sd, n - 1)
                    pe.matmul(bank[6 + J % 2][:, 0:S - J * P], RK[:, h, J * P:(J + 1) * P], RQ[:, h, J * P:S],
                              start=True, stop=True).then_inc(r_s, 1)
                if J:
                    K = J - 1
                    pe.wait_ge(r_sd, 4 * h + K + 1)
                    if K == 0 and h:
                        pe.wait_ge(r_oc, h)
                    for vb in range(2):
                        mm = pe.matmul(bank[2 + vb][:, K * P:S], RV[:, K, h * 256 + vb * P:h * 256 + (vb + 1) * P],
                                       RSC[:, K % 2, 0:S - K * P], start=(K == 0), stop=(K == TB - 1),
                                       skip_group_check=True)
                    mm.then_inc(r_pv, 1)

            for it in range(2):
                for n in range(16 + 3):
                    if n < 16:
                        at2_scores(n, it)
                    for hh in range(2):
                        if 0 <= n - RET_AT[hh] <= TB:
                            ret_step(2 * it + hh, n - RET_AT[hh])
                    if 2 <= n < 18:
                        at2_turn(n - 2, it)
                    if n >= 3:
                        at2_values(n - 3, it)
            pe.wait_ge(at_lo, 64)
            for h in range(4):
                pe.wait_ge(r_oc, h + 1)
                for vb in range(2):
                    mm = pe.matmul(bank[4 + h][:, :], ones[:, :], OT[:, 2 * h + vb, :], start=(vb == 0), stop=(vb == 1))
                mm.then_inc(gn_mu, 1)
            for h in range(4):
                pe.wait_ge(gn_sq, 2 * h + 2)
                for vb in range(2):
                    mm = pe.matmul(bank[4 + h][:, :], ones[:, :], T[:, 2 * h + vb, :], start=(vb == 0), stop=(vb == 1))
                mm.then_inc(gn_var, 1)

            def columns2(name, n):
                with pe.Fori(0, n // 4) as i:
                    for u in range(4):
                        t = G0[name] + u
                        columns(i * 4 + t, t % R, i * 4 + (t - e0)).then_inc(tile_done, 1)

            pe.wait_ge(r_oc, 4)
            columns2("rg", 8)
            columns2("ga2", 8)
            pe.wait_ge(gn_root, 4)
            for u in range(4):
                g = G0["atto"] + u
                narrow(g, g % R, g - e0, ATH, ATL)
            columns2("gr2", 8)
            pe.wait_ge(rg_lo, 8)
            layer("reto", None, e0, RH, RL)
            layer("out2", (mg_lo, KB), e0)
            norm_sum(S)
            layer("gateup", (n_lo, 4 * KB), e0)
            pe.wait_ge(tile_evac, evac_before(G0["down"]))

            def down(f, t, first=False, last=False):
                pe.wait_ge(w_lo, f + (G0["down"] + 1))
                pe.wait_ge(ff_lo, f + 1)
                xh = FH[:, bass.ds(f, 1), :].rearrange("p o t -> p (o t)")
                xl = FL[:, bass.ds(f, 1), :].rearrange("p o t -> p (o t)")
                add_up(t % R, xh, xl, first, last)

            down(0, G0["down"], first=True)
            with pe.Fori(0, (FB - 2) // 4) as i:
                for u in range(4):
                    down(i * 4 + (1 + u), G0["down"] + 1 + u)
            down(FB - 1, G0["down"] + FB - 1, last=True)
            norm_sum(S, 0)

        @block.vector
        def _(v):
            chain = Tally()

            def then(ins):
                ins.then_inc(dve, 1)
                chain.add()
                v.wait_ge(dve, chain.at())

            scaled = [0, 0, 0]

            def norm_rstd(width):
                scaled[0] += 1
                v.wait_ge(n_root, scaled[0])
                then(nc.vector.reciprocal(rstd[:, 0:width], rms[:, 0:width]))

            def norm_scale(src, width, gain, dst=T):
                for kb in range(KB):
                    nc.vector.scalar_tensor_tensor(dst[:, kb, 0:width], src[:, kb, :], gain(kb), rstd[:, 0:width],
                                                   ALU.mult, ALU.mult).then_inc(n_scaled, 1)

            def norm_low(width, H, L, shift=None):
                for kb in range(KB):
                    scaled[2] += 1
                    v.wait_ge(n_hi, scaled[2])
                    h = H[:, kb, :].bitcast(F32)
                    if shift is None:
                        ins = nc.vector.tensor_tensor(L[:, kb, :], T[:, kb, 0:width], h, ALU.subtract)
                    else:
                        ins = nc.vector.scalar_tensor_tensor(L[:, kb, :], T[:, kb, 0:width], shift(kb), h, ALU.add,
                                                             ALU.subtract)
                    ins.then_inc(n_lo, 1)

            def row_sum(tile, sc, products, a, who):
                return nc.vector.tensor_tensor_reduce(products, tile, sc, 1.0, 0.0, ALU.mult, ALU.add,
                                                       mod[:, a, who:who + 1])

            def add_bias(a0, n, who):
                m = mod[:, a0:a0 + n, who]
                a = COLS["adab"][0] + a0
                then(nc.vector.tensor_tensor(m, m, cols[:, a:a + n], ALU.add))

            def gain_scale(k, chunk, who, name):
                a, b = COLS[name]
                nc.vector.scalar_tensor_tensor(gsc[:, k, :], mod[:, chunk:chunk + 8, who], 1.0, cols[:, a:b], ALU.add,
                                               ALU.mult).then_inc(gsc_ready, 1)

            nc.vector.memset(eps[:, :], EPS).then_inc(n_eps, 1)
            v.wait_ge(silu_c, 1)
            for a in range(16):
                if a == 11:
                    norm_rstd(S)
                v.wait_ge(ada1_in[a], 16)
                if a >= 2:
                    v.wait_ge(ada_used, a - 1)
                row_sum(ada1[:, a, :], sc2[:, 0, :], junk[:, a % 2, :], a, 0).then_inc(ada_used, 1)
            v.wait_ge(ada_used, 16)
            add_bias(0, 16, 0)
            gain_scale(0, 8, 0, "n1")
            v.wait_ge(gsc_ready, 1)
            norm_scale(X, S, lambda kb: gsc[:, 0, kb:kb + 1])
            norm_low(S, HH, HL, lambda kb: mod[:, kb, 0:1])
            for a in range(KB, 16):
                ins = row_sum(ada1[:, a, :], sc2[:, 1, :], ada1[:, a, :], a, 1)
            then(ins)
            v.wait_ge(ada_ctx, KB)
            add_bias(0, 16, 1)
            gain_scale(1, 8, 1, "n1")

            def copy_tile(g, dst, src):
                v.wait_ge(tile_done, g + 1)
                return nc.vector.tensor_copy(dst, src)

            for u in range(2):
                copy_tile(u, QT[:, u, :], bank[u][:, :]).then_inc(tile_evac, 1)
            norm_rstd(CTX)
            v.wait_ge(gsc_ready, 2)
            norm_scale(CX, CTX, lambda kb: gsc[:, 1, kb:kb + 1])
            norm_low(CTX, CH, CL, lambda kb: mod[:, kb, 1:2])
            for u in range(2, 4):
                copy_tile(u, QT[:, u, :], bank[u][:, :]).then_inc(tile_evac, 1)
            for u in range(4):
                copy_tile(G0["k"] + u, KT[:, u, 0:S], bank[u][:, :])
                nc.vector.tensor_copy(KT[:, u, S:S + CTX], bank[4 + u][:, 0:CTX]).then_inc(tile_evac, 1)
            v.wait_ge(tile_done, G0["gu"])
            for b in range(6):
                ins = nc.vector.tensor_copy(VV[:, b, :], bank[b][:, :])
                if b >= 2:
                    ins.then_inc(tile_evac, 1)

            v.wait_ge(late_in, 16)

            def at1_mask(n, it):
                pair, hh, a = n // 8, n // 4 % 2, n % 4
                b = n % 2
                if n % 8 == 0:
                    v.wait_ge(bias_in[pair], it * 64 + 64)
                    for k in range(2):
                        e3 = E[:, pair, k, :].rearrange("p (m k) -> p m k", k=HD)
                        ins = nc.vector.tensor_tensor(e3, e3, bc(wmask[:, :], 1, 14), ALU.add)
                    then(ins)
                v.wait_ge(at_s, it * 16 + (n + 1))
                if n >= 3:
                    v.wait_ge(at_t, it * 16 + (n - 2))
                m0, c = (6 - 2 * a) * HD, n % 3
                nc.vector.scalar_tensor_tensor(SS[:, c, 0:S], bank[4 + 2 * b][:, :], SCALE, E[:, pair, hh, m0:m0 + S],
                                               ALU.mult, ALU.add)
                then(nc.vector.tensor_scalar(SS[:, c, S:S + CTX], bank[5 + 2 * b][:, 0:CTX], SCALE, None, ALU.mult))
                nc.vector.tensor_reduce(mx[:, c, 0:1], SS[:, c, :], AX_X, ALU.max, negate=True).then_inc(at_masked, 1)

            def at1_prob(n, it):
                c = n % 3
                v.wait_ge(at_exp, it * 16 + (n + 1))
                then(nc.vector.reciprocal(mx[:, c, 2:3], mx[:, c, 1:2]))
                nc.vector.tensor_scalar(SS[:, c, :], SS[:, c, :], mx[:, c, 2:3], None, ALU.mult).then_inc(at_p, 1)

            def at1_low(n, it):
                pair, hh, a = n // 8, n // 4 % 2, n % 4
                v.wait_ge(at_hi, it * 16 + (n + 1))
                r = slice(64 * hh, 64 * hh + 64)
                dst = YAL[r, bass.ds(it * 2 + pair, 1), a * P:(a + 1) * P].rearrange("p o q -> p (o q)")
                h = YAH[r, bass.ds(it * 2 + pair, 1), a * P:(a + 1) * P].rearrange("p o q -> p (o q)").bitcast(F32)
                nc.vector.tensor_tensor(dst, bank[2 * (n % 2) + 1][r, 256:384], h, ALU.subtract).then_inc(at_lo, 1)

            chain_loop(v, chain, 2, 2 + 16 * 2, lambda it: [
                (at1_mask(n, it) if n < 16 else None, at1_prob(n - 1, it) if 1 <= n <= 16 else None,
                 at1_low(n - 3, it) if n >= 3 else None) for n in range(16 + 3)])

            v.wait_ge(silu_c, 2)

            def ada_rows(a0, a1):
                for a in range(a0, a1):
                    v.wait_ge(ada_in[a % R], 16 * (a // R - 3))
                    row_sum(adaw[:, a % R, :], sc_row, adaw[:, a % R, :], a, 0).then_inc(ada_used, 1)

            ada_rows(16, 32)
            v.wait_ge(tile_evac, G0["gates"])
            for tb in range(TB):
                ins = nc.vector.bn_stats(bn[:, tb, :], GV[:, tb, :])
            then(ins)
            for tb in range(TB):
                ins = nc.vector.bn_aggr(st[:, 2 * tb + 16:2 * tb + 18], bn[:, tb, :])
            then(ins)
            for tb in range(TB):
                nc.vector.tensor_copy(st[:, 4 + tb:5 + tb], st[:, 2 * tb + 17:2 * tb + 18]).then_inc(gm_var, 1)
            v.wait_ge(gm_root, 1)
            then(nc.vector.reciprocal(st[:, 12:16], st[:, 8:12]))
            for tb in range(TB):
                nc.vector.tensor_scalar(GV[:, tb, :], GV[:, tb, :], st[:, 2 * tb + 16:2 * tb + 17],
                                        st[:, 12 + tb:13 + tb], ALU.subtract, ALU.mult).then_inc(gm_vn, 1)
            ada_rows(32, 48)
            v.wait_ge(ada_used, 48)
            add_bias(16, 32, 0)
            gain_scale(2, 32, 0, "n2")
            v.wait_ge(gm_mix, 1)
            v.wait_ge(late_in, 48)
            for b in range(4):
                then(nc.vector.scalar_tensor_tensor(
                    MX[:, b, :].rearrange("p (c q) -> p c q", c=TB), bank[4 + b][:, :].rearrange("p (c q) -> p c q", c=TB),
                    col("lng", b), bc(bsb[:, b, :], 1, TB), ALU.mult, ALU.add))
                nc.vector.tensor_tensor(MX[:, b, :], MX[:, b, :], UT[:, b, :], ALU.mult).then_inc(gm_y, 1)
            for b in range(4):
                v.wait_ge(gm_hi, b + 1)
                nc.vector.tensor_tensor(YBL[:, b, :], MX[:, b, :], YBH[:, b, :].bitcast(F32), ALU.subtract)\
                    .then_inc(gm_lo, 1)
            v.wait_ge(tile_evac, G0["pa"])
            v.wait_ge(gm_lo, 4)
            for u in range(4):
                v.wait_ge(tile_done, G0["pa"] + u + 1)
                nc.vector.tensor_tensor(T[:, 2 * u, :], bank[u][:, :], SG[:, 2 * u, :], ALU.mult)
                nc.vector.tensor_tensor(T[:, 2 * u + 1, :], bank[4 + u][:, :], SG[:, 2 * u + 1, :], ALU.mult)\
                    .then_inc(tile_evac, 1)

            def split_merged(k, h0):
                v.wait_ge(mg_hi, h0 + k + 1)
                nc.vector.tensor_tensor(HL[:, k, :], T[:, k, :], HH[:, k, :].bitcast(F32), ALU.subtract)\
                    .then_inc(mg_lo, 1)

            for u in range(4):
                v.wait_ge(tile_done, G0["pb"] + u + 1)
                nc.vector.tensor_tensor(SG[:, 8 + 2 * u, :], bank[u][:, :], SG[:, 8 + 2 * u, :], ALU.mult)
                ins = nc.vector.tensor_tensor(SG[:, 9 + 2 * u, :], bank[4 + u][:, :], SG[:, 9 + 2 * u, :], ALU.mult)
                ins.then_inc(tile_evac, 1)
                v.wait_ge(tile_evac, G0["pb"] + u + 1)
                for k in (2 * u, 2 * u + 1):
                    nc.vector.tensor_tensor(T[:, k, :], T[:, k, :], SG[:, 8 + k, :], ALU.add).then_inc(mg_m, 1)
                if u:
                    split_merged(2 * u - 2, 0)
                    split_merged(2 * u - 1, 0)
            split_merged(6, 0)
            split_merged(7, 0)

            def residual(ps, kb, gate):
                xk = X[:, kb, :]
                if gate is None:
                    return nc.vector.tensor_tensor(xk, ps, xk, ALU.add)
                return nc.vector.scalar_tensor_tensor(xk, ps, gate, xk, ALU.mult, ALU.add)

            for k in range(8):
                v.wait_ge(tile_done, G0["out"] + k + 1)
                residual(bank[k % R][:, :], k, mod[:, 16 + k, 0:1]).then_inc(tile_evac, 1)
            norm_rstd(S)
            v.wait_ge(gsc_ready, 3)
            norm_scale(X, S, lambda kb: gsc[:, 2, kb:kb + 1])
            norm_low(S, HH, HL, lambda kb: mod[:, 24 + kb, 0:1])

            def topk(tb):
                v.wait_ge(sc_evac, tb * 4 + 4)
                then(nc.vector.tensor_copy(SSc, SC[:, tb, :, :]))

                def sixteen(lists, values, indices, count):
                    for n in range(count):
                        ins = nc.vector.max(values(n)[:, 0:8], lists(n))
                    then(ins)
                    for n in range(count):
                        ins = nc.vector.max_index(indices(n)[:, 0:8], values(n)[:, 0:8], lists(n))
                    then(ins)
                    for n in range(count):
                        ins = nc.vector.match_replace(lists(n), values(n)[:, 0:8], lists(n), MASKED)
                    then(ins)
                    for n in range(count):
                        ins = nc.vector.max(values(n)[:, 8:16], lists(n))
                    then(ins)
                    for n in range(count):
                        ins = nc.vector.max_index(indices(n)[:, 8:16], values(n)[:, 8:16], lists(n))
                    then(ins)

                sixteen(lambda n: SSc[:, n, :], lambda n: small[:, n, :], lambda n: tki[:, n, :], 16)
                nc.vector.tensor_copy(tkf[:, :, :], tki[:, :, :])
                halves = small[:, :, :].rearrange("p (h w) a -> p w h a", w=2)
                then(nc.vector.tensor_tensor(cand, bc(halves[:, 0], 3, 16), bc(halves[:, 1], 2, 16), ALU.add))
                c2 = cand.rearrange("p h a b -> p h (a b)")
                sixteen(lambda h: c2[:, h, :], lambda h: bv[:, h, :], lambda h: bp[:, h, :], NH)
                nc.vector.tensor_scalar(bab[:, 0, :, :], bp[:, :, :], 4, None, ALU.logical_shift_right)
                nc.vector.tensor_scalar(bab[:, 1, :, :], bp[:, :, :], 15, None, ALU.bitwise_and)
                then(nc.vector.tensor_copy(hs[:, 1, :], bv[:, :, 0]))
                nc.vector.tensor_tensor(bv[:, :, :], bv[:, :, :], bc(hs[:, 1, :], 2, 16), ALU.subtract)\
                    .then_inc(tk_diff, 1)
                then(nc.vector.tensor_copy(babf[:, :, :, :], bab[:, :, :, :]))
                idx = tkf[:, :, :].rearrange("p (h w) a -> p w h a", w=2)
                iota16 = bc(bc(iota[:, 0:16], 1, 16), 1, NH)
                for w in range(2):
                    then(nc.vector.tensor_tensor(cand, bc(babf[:, w, :, :], 3, 16), iota16, ALU.is_equal))
                    then(nc.vector.tensor_tensor(cand, cand, bc(idx[:, w], 2, 16), ALU.mult))
                    ins = nc.vector.tensor_reduce(sel3[:, w, :].rearrange("p (h k) -> p h k", h=NH), cand, AX_X,
                                                  ALU.add)
                    then(ins)
                v.wait_ge(tk_exp, tb + 1)
                then(nc.vector.tensor_reduce(hs[:, 0, :], bv[:, :, :], AX_X, ALU.add))
                then(nc.vector.reciprocal(hs[:, 1, :], hs[:, 0, :]))
                nc.vector.tensor_tensor(sel3[:, 2, :].rearrange("p (h k) -> p h k", h=NH), bv[:, :, :],
                                        bc(hs[:, 1, :], 2, 16), ALU.mult).then_inc(tk_sel, 1)
                v.wait_ge(tk_tr, tb + 1)
                nc.vector.tensor_copy(IT[:, :, tb * P:(tb + 1) * P], bank[4][:, 0:3 * P].rearrange("p (k t) -> p k t", k=3))\
                    .then_inc(tk_it, 1)

            v.wait_ge(const2_in, 32)
            v.wait_ge(keys_in, 16)
            v.wait_ge(sc_done, 16)
            for tb in range(TB):
                topk(tb)
            v.wait_ge(tk_it, TB)
            then(nc.vector.tensor_copy(GH[:, :], IT[:, 2, :]))
            nc.vector.tensor_tensor(IT[:, 2, :], IT[:, 2, :], GH[:, :].bitcast(F32), ALU.subtract).then_inc(tk_gate, 1)
            v.wait_ge(tk_gate, 1)

            def onehots(q, peeled=False):
                rings = (slice(0, 4), slice(4, 8))
                for half in range(2):
                    if not peeled:
                        v.wait_ge(g_done, q + (half - 1))
                        v.wait_ge(oh_low, q + (half - 1))
                    nc.vector.tensor_tensor(OJ[:, rings[half], :], bc(iota[:, :], 1, 4),
                                            bc(IT[:, 1, bass.ds(q * 4 + 4 * half, 4)], 2, P), ALU.is_equal)\
                        .then_inc(oh_j, 1)
                for half in range(2):
                    v.wait_ge(oh_j, q + (half + 1))
                    nc.vector.tensor_tensor(OG[:, rings[half], 0, :], OJ[:, rings[half], :],
                                            bc(GH[:, bass.ds(q * 4 + 4 * half, 4)].bitcast(F32), 2, P), ALU.mult)
                    nc.vector.tensor_tensor(OI[:, rings[half], :], bc(iota[:, :], 1, 4),
                                            bc(IT[:, 0, bass.ds(q * 4 + 4 * half, 4)], 2, P), ALU.is_equal)\
                        .then_inc(oh_ready, 1)

            def g_sum(q, m):
                for k in range(2):
                    v.wait_ge(g_high, q * 2 + (k + 1))
                    t = 4 * (m % 16) + 2 * k
                    low = bank[4 + 2 * (m % 2) + k][:, :].rearrange("p (t w j) -> p w j t", t=2, w=2)[:, 1]
                    g = GS[:, m // 16, :, t:t + 2]
                    ins = nc.vector.tensor_tensor(g, low, g, ALU.add)
                ins.then_inc(g_evac, 1)

            def gate_blocks(i, first):
                for n in range(0, 32, 2):
                    onehots(i * 32 + n, peeled=(first and n == 0))
                    for k in range(2):
                        if n or not first:
                            g_sum(i * 32 + (n + k - 2), (n + k - 2) % 32)

            gate_blocks(0, True)
            with v.Fori(1, 4) as i:
                gate_blocks(i, False)
            for m in (30, 31):
                g_sum(96 + m, m)

            def pw_tile(j, slot, turns, peeled=False):
                v.wait_ge(ag_in[slot], turns)
                if not peeled:
                    v.wait_ge(tile_done, j + (G0["V"] - R + 1))
                nc.vector.tensor_tensor(AJ[:, slot, :], AJ[:, slot, :],
                                        GJ[:, slot, :, :].rearrange("p b t -> p (b t)"), ALU.mult).then_inc(pw, 1)
                v.wait_ge(pw_hi, j + 1)
                nc.vector.tensor_tensor(WL[:, slot, :], AJ[:, slot, :], WH[:, slot, :].bitcast(F32), ALU.subtract)\
                    .then_inc(pw_lo, 1)

            for u in range(4):
                pw_tile(u, u, 32, peeled=True)
            with v.Fori(1, 32) as i:
                for u in range(4):
                    pw_tile(i * 4 + u, u, i * 32 + 32)
            v.wait_ge(tile_done, G0["aq"])
            for kb in range(KB):
                residual(bank[kb][:, :], kb, mod[:, 40 + kb, 0:1]).then_inc(res_done, 1)

            v.wait_ge(res_done, KB)
            norm_rstd(S)
            norm_scale(X, S, lambda kb: col("fin1", kb), X)
            norm_rstd(S)
            norm_scale(X, S, lambda kb: col("mix2", kb))
            norm_low(S, HH, HL)
            for k in range(4):
                v.wait_ge(tile_done, G0["aq"] + k + 1)
                nc.vector.tensor_scalar(AQ[:, k, :], bank[k][:, :], SCALE, None, ALU.mult).then_inc(tile_evac, 1)
            for k in range(4):
                copy_tile(G0["rq"] + k, RQ[:, k, :], bank[k][:, :]).then_inc(tile_evac, 1)
            for k in range(4):
                v.wait_ge(tile_done, G0["rk"] + k + 1)
                nc.vector.tensor_scalar(RK[:, k, :], bank[k][:, :], P ** -0.5, None, ALU.mult).then_inc(tile_evac, 1)
            for h in range(2):
                for b in range(TB):
                    copy_tile(G0["rv"] + 4 * h + 3, RV[:, b, h * S:(h + 1) * S], bank[4 - 4 * h + b][:, :])\
                        .then_inc(tile_evac, 1)
            copy_tile(G0["av"], AVT[:, :], bank[0][:, :]).then_inc(tile_evac, 1)
            copy_tile(G0["ak"], AK[:, :], bank[1][:, :]).then_inc(tile_evac, 1)
            v.wait_ge(av_turned, 1)
            nc.vector.tensor_copy(AV[:, :, :], bank[7][:, :].rearrange("p (b c) -> p b c", b=TB)).then_inc(av_ready, 1)

            v.wait_ge(alibi_in, 16)

            def at2_mask(n, it):
                m, r, a = n // 8, n // 4 % 2, n % 4
                b, c = n % 2, n % 3
                v.wait_ge(at_s, it * 16 + (32 + n + 1))
                if n >= 3:
                    v.wait_ge(at_t, it * 16 + (32 + n - 2))
                k0 = 0 if a else P
                if not a:
                    nc.vector.memset(AS[:, c, 0:P], NEG)
                slope = cols[:, bass.ds(it * 4 + (COLS["slope"][0] + 2 * m + r), 1)]
                sink = cols[:, bass.ds(it * 4 + (COLS["sink"][0] + 2 * m + r), 1)]
                then(nc.vector.scalar_tensor_tensor(AS[:, c, k0:256], alibi[:, k0:256], slope, bank[4 + b][:, k0:256],
                                                    ALU.mult, ALU.add))
                then(nc.vector.tensor_reduce(amx[:, c, 5:6], AS[:, c, :], AX_X, ALU.max))
                then(nc.vector.tensor_scalar(amx[:, c, 0:1], amx[:, c, 5:6], sink, -1.0, ALU.max, ALU.mult))
                nc.vector.tensor_tensor(amx[:, c, 2:3], amx[:, c, 0:1], sink, ALU.add).then_inc(at_masked, 1)

            def at2_prob(n, it):
                c = n % 3
                v.wait_ge(at_exp, it * 32 + (32 + 2 * n + 2))
                then(nc.vector.tensor_tensor(amx[:, c, 5:6], amx[:, c, 1:2], amx[:, c, 3:4], ALU.add))
                then(nc.vector.reciprocal(amx[:, c, 6:7], amx[:, c, 5:6]))
                nc.vector.tensor_scalar(AS[:, c, :], AS[:, c, :], amx[:, c, 6:7], None, ALU.mult).then_inc(at_p, 1)

            def at2_low(n, it):
                m, r, a = n // 8, n // 4 % 2, n % 4
                v.wait_ge(at_hi, it * 16 + (32 + n + 1))
                rr = slice(64 * r, 64 * r + 64)
                dst = ATL[rr, bass.ds(it * 2 + m, 1), a * P:(a + 1) * P].rearrange("p o q -> p (o q)")
                h = ATH[rr, bass.ds(it * 2 + m, 1), a * P:(a + 1) * P].rearrange("p o q -> p (o q)").bitcast(F32)
                nc.vector.tensor_tensor(dst, bank[n % 2][rr, 256:384], h, ALU.subtract).then_inc(at_lo, 1)

            def ret_decay(hh, J, it):
                if J == 0:
                    v.wait_ge(dec_in, it * 32 + 16 * (hh + 1))
                n = 4 * hh + J
                v.wait_ge(r_s, it * 8 + (n + 1))
                if n >= 2:
                    v.wait_ge(r_pv, it * 8 + (n - 1))
                nc.vector.tensor_tensor(RSC[:, J % 2, 0:S - J * P], bank[6 + J % 2][:, 0:S - J * P],
                                        DEC[:, 0:S - J * P], ALU.mult).then_inc(r_sd, 1)

            def ret_out(hh, it):
                v.wait_ge(r_pv, it * 8 + (4 * hh + 4))
                for vb in range(2):
                    ins = nc.vector.tensor_copy(OT[:, bass.ds(it * 4 + (2 * hh + vb), 1), :].rearrange("p o t -> p (o t)"),
                                                bank[2 + vb][:, :])
                ins.then_inc(r_oc, 1)

            def at2_loop(it):
                for n in range(16 + 3):
                    if n < 16:
                        at2_mask(n, it)
                    for hh in range(2):
                        J = n - RET_AT[hh]
                        if 0 <= J < TB:
                            ret_decay(hh, J, it)
                        elif J == TB + 1:
                            ret_out(hh, it)
                    if 1 <= n <= 16:
                        at2_prob(n - 1, it)
                    if n >= 3:
                        at2_low(n - 3, it)

            chain_loop(v, chain, 2, 16 * 5, at2_loop)
            for h in range(4):
                v.wait_ge(gn_mu, h + 1)
                for vb in range(2):
                    o = OT[:, 2 * h + vb, :]
                    nc.vector.scalar_tensor_tensor(o, bank[4 + h][:, :], -1.0 / 256, o, ALU.mult, ALU.add)\
                        .then_inc(gn_cen, 1)
            for h in range(4):
                v.wait_ge(gn_root, h + 1)
                then(nc.vector.reciprocal(rst4[:, h, :], rst4[:, h, :]))
                for vb in range(2):
                    k = 2 * h + vb
                    nc.vector.scalar_tensor_tensor(OT[:, k, :], OT[:, k, :], col("gn", k), rst4[:, h, :], ALU.mult,
                                                   ALU.mult).then_inc(gn_done, 1)
            for k in range(8):
                v.wait_ge(tile_evac, evac_before(G0["rg"]) + k + 1)
                if k == 0:
                    v.wait_ge(gn_done, 8)
                nc.vector.tensor_tensor(T[:, k, :], T[:, k, :], OT[:, k, :], ALU.mult).then_inc(rg_mul, 1)
                v.wait_ge(rg_hi, k + 1)
                nc.vector.tensor_tensor(RL[:, k, :], T[:, k, :], RH[:, k, :].bitcast(F32), ALU.subtract)\
                    .then_inc(rg_lo, 1)
            for u in range(4):
                g = G0["atto"] + u
                v.wait_ge(tile_done, g + 1)
                if u == 0:
                    v.wait_ge(tile_evac, evac_before(g))
                nc.vector.tensor_tensor(T[:, 2 * u, :], bank[g % R][:, :], T[:, 2 * u, :], ALU.mult)
                nc.vector.tensor_tensor(T[:, 2 * u + 1, :], bank[4 + g % R][:, :], T[:, 2 * u + 1, :], ALU.mult)\
                    .then_inc(tile_evac, 1)
            for k in range(8):
                g = G0["reto"] + k
                v.wait_ge(tile_done, g + 1)
                v.wait_ge(tile_evac, evac_before(g))
                nc.vector.tensor_tensor(OT[:, k, :], bank[g % R][:, :], OT[:, k, :], ALU.mult).then_inc(tile_evac, 1)
                v.wait_ge(tile_evac, evac_before(g) + 1)
                nc.vector.tensor_tensor(T[:, k, :], T[:, k, :], OT[:, k, :], ALU.add).then_inc(mg_m, 1)
                if k:
                    split_merged(k - 1, KB)
            split_merged(7, KB)
            for k in range(8):
                g = G0["out2"] + k
                v.wait_ge(tile_done, g + 1)
                residual(bank[g % R][:, :], k, None).then_inc(tile_evac, 1)
            norm_rstd(S)
            norm_scale(X, S, lambda kb: col("ffn2", kb))
            norm_low(S, HH, HL)
            with v.Fori(0, FB // 2) as i:
                for k in range(2):
                    t = G0["gateup"] + 2 * k
                    v.wait_ge(tile_done, i * 4 + (t + 2))
                    v.wait_ge(tile_evac, i * 4 + (evac_before(t) + 1))
                    nc.vector.tensor_tensor(T[:, k, :], bank[(t + 1) % R][:, :], T[:, k, :], ALU.mult)\
                        .then_inc(ff_mul, 1)
                    v.wait_ge(tile_evac, i * 4 + (evac_before(t) + 2))
                    nc.vector.tensor_tensor(FL[:, bass.ds(i * 2 + k, 1), :].rearrange("p o t -> p (o t)"), T[:, k, :],
                                            FH[:, bass.ds(i * 2 + k, 1), :].rearrange("p o t -> p (o t)").bitcast(F32),
                                            ALU.subtract).then_inc(ff_lo, 1)
            v.wait_ge(tile_done, NT)
            for kb in range(KB):
                residual(bank[kb][:, :], kb, None).then_inc(res_done, 1)
            v.wait_ge(res_done, 2 * KB)
            norm_rstd(S)
            norm_scale(X, S, lambda kb: col("fin2", kb))


def pack_tiles(inp):
    import numpy as np

    def blocks(w):
        k, n = w.shape
        return w.reshape(k // P, P, n // P, P).transpose(2, 1, 0, 3)

    def full(w):
        return blocks(w).reshape(-1, P, D)

    def half(w):
        b = blocks(w)
        return b.reshape(b.shape[0] // 2, 2, P, 4, P).transpose(0, 2, 1, 3, 4).reshape(-1, P, D)

    w1 = inp["w_in"][0]
    a, g = NH * HD, 512
    cuts = dict(q=w1[:, 0:a], k=w1[:, a:2 * a], v=w1[:, 2 * a:3 * a], gu=w1[:, 3 * a:3 * a + g],
                gv=w1[:, 3 * a + g:3 * a + 2 * g], gates=w1[:, 3 * a + 2 * g:])
    w2 = inp["w_in_2"][0]
    names = [("aq", 512), ("ak", 128), ("av", 128), ("rq", 512), ("rk", 512), ("rv", 1024), ("rg", 1024),
             ("ga2", 1024), ("gr2", 1024)]
    at = 0
    for name, n in names:
        cuts[name] = w2[:, at:at + n]
        at += n
    cuts["aq"] = cuts["aq"].reshape(D, 2, 4, HD).transpose(0, 2, 1, 3).reshape(D, 512)
    atto = inp["w_att_o_2"][0].reshape(2, 4, HD, D).transpose(1, 0, 2, 3).reshape(512, D)
    def pairs(w):
        return w.reshape(4, 2, P, -1, S).transpose(3, 0, 2, 1, 4).reshape(-1, P, D)

    parts = {name: (pairs if name in ("v", "gv", "rv") else full)(w) for name, w in cuts.items()}
    parts["pa"], parts["pb"], parts["atto"] = half(inp["w_proj_a"][0]), half(inp["w_proj_b"][0]), half(atto)
    parts["out"], parts["out2"], parts["reto"] = (full(inp[n][0]) for n in ("w_out", "w_out_2", "w_ret_o_2"))
    parts["wq"] = full(inp["peer_wq"][0])
    parts["U"] = inp["peer_u"][0].reshape(P, P, KB, P).transpose(1, 3, 2, 0).reshape(P, P, D)
    parts["V"] = inp["peer_v"][0].reshape(P, P, D).transpose(1, 0, 2)
    gate, up = full(inp["w_gate_2"][0]), full(inp["w_up_2"][0])
    parts["gateup"] = np.stack([gate, up], 1).reshape(-1, P, D)
    parts["down"] = inp["w_down_2"][0].reshape(FB, P, D)
    for name, n in PARTS:
        assert parts[name].shape == (n, P, D), (name, parts[name].shape)
    return np.concatenate([parts[name] for name, _ in PARTS])


def feature_rows(x):
    return x.reshape(x.shape[0], -1, P).transpose(2, 1, 0)


def pack(inp):
    import numpy as np

    f = np.float32

    def col(v):
        return v.reshape(-1, P).T

    sinks = inp["att_sinks_2"][0].reshape(2, 4).T.reshape(-1)
    slopes = (2.0 ** (-8.0 * (np.arange(8) + 1.0) / 8)).astype(f).reshape(2, 4).T.reshape(-1)
    tables = dict(n1=col(inp["norm1_g"][0]), n2=col(inp["norm2_g"][0]), fin1=col(inp["final_g"]),
                  mix2=col(inp["norm_mix_2"][0]), ffn2=col(inp["norm_ffn_2"][0]), fin2=col(inp["final_norm_2"]),
                  adab=col(inp["ada_b"][0]), lng=col(inp["gm_ln_g"][0]), gn=col(inp["ret_gn_gain_2"][0]),
                  sink=np.broadcast_to(sinks, (P, 8)), slope=np.broadcast_to(slopes, (P, 8)))
    rpb = np.zeros((8, 15, 127), f)
    rpb[:, :, 48:79] = inp["na_rpb"][0]
    qc, kc = np.arange(HD)[:, None], np.arange(HD)[None, :]
    start = np.clip(qc - 8, 0, HD - 16)
    window = np.where((kc >= start) & (kc < start + 16), 0.0, NEG).astype(f)
    i, j = np.arange(P)[:, None], np.arange(2 * P)[None, :]
    dist = i + P - j
    alibi = np.where((dist >= 0) & (dist < P), -dist, NEG).astype(f)
    ahead = np.arange(S)[None, :] - np.arange(P)[:, None]
    dec = np.stack([np.where(ahead >= 0, (1.0 - 2.0 ** (-5 - h)) ** np.maximum(ahead, 0), 0.0) for h in range(4)])
    bs = np.repeat(inp["gm_bs"][0].reshape(4, 2, 1, P), HD, axis=2)
    return dict(
        w=pack_tiles(inp),
        ada=inp["ada_w"][0].T.reshape(48, P, D),
        x=feature_rows(inp["x"][0]), ctx=feature_rows(inp["ctx"][0]),
        c=np.stack([inp["c"][0], inp["c_ctx"].reshape(D)]),
        cols=np.concatenate([tables[n] for n in COLS], 1), ones=np.ones((P, P), f), ident=np.eye(P, dtype=f),
        iota=np.broadcast_to(np.arange(P, dtype=f), (P, P)), wmask=np.concatenate([window, window]), alibi=alibi,
        dec=dec.astype(f), rpb=np.broadcast_to(rpb, (HD, 8, 15, 127)), wsT=inp["gm_ws"][0].transpose(2, 0, 1),
        bs=bs.reshape(4, P, P).transpose(1, 0, 2), keys=inp["peer_keys"][0].reshape(16, P, P).transpose(2, 0, 1))


def kernel(**inputs):
    import numpy as np
    import concourse.bacc as bacc
    from concourse.bass_utils import run_bass_kernel_spmd

    nc = bacc.Bacc("TRN2", target_bir_lowering=False, num_devices=1)
    arrays, aps = {}, {}
    for name, a in pack({k: np.asarray(v) for k, v in inputs.items()}).items():
        a = np.ascontiguousarray(a)
        arrays[f"in_{name}"] = a
        aps[name] = nc.dram_tensor(f"in_{name}", a.shape, mybir.dt.from_np(a.dtype), kind="ExternalInput").ap()
    out = nc.dram_tensor("out_0", (P, KB, S), F32, kind="ExternalOutput").ap()
    build(nc, aps, out)
    r = run_bass_kernel_spmd(nc, [arrays], core_ids=[0])
    return r.results[0]["out_0"].transpose(2, 1, 0).reshape(1, S, D)
```
